# Optimizing a Trainium2 kernel written in Bass

```python
import jax, jax.numpy as jnp
from jax import lax
import numpy as np

D_MODEL = 1024
BATCH = 1
SEQ = 2048
DEPTH = 2
DEC_BATCH = 1
DEC_SEQ = 64
PAST_LEN = 2048

CHUNK = 64
N_A_LAYERS = DEPTH // 2
N_B_LAYERS = DEPTH - N_A_LAYERS
D_RNN = D_MODEL
GATE_BLOCK = 256
N_GATE_BLOCKS = D_RNN // GATE_BLOCK
CONV_W = 4
LRU_C = 8.0
HEAD_DIM = 64
N_HEADS = D_MODEL // HEAD_DIM
N_KV = 2
GROUP = N_HEADS // N_KV
WINDOW = 128
WIN_CHUNKS = WINDOW // CHUNK
EPS = 1e-6
NEG = -1e30

kernel_name = "yoco_rglru_swa_sink_stream_step"

def _rmsnorm(x, g):
    xf = x.astype(jnp.float32)
    y = xf * lax.rsqrt(jnp.mean(xf * xf, axis=-1, keepdims=True) + EPS)
    return (y * g.astype(jnp.float32)).astype(x.dtype)

def _causal_conv(u, buf, w, b):
    t = u.shape[1]
    up = jnp.concatenate([buf.astype(u.dtype), u], axis=1)
    out = b
    for j in range(CONV_W):
        out = out + w[j] * up[:, j:j + t]
    return out, up[:, -(CONV_W - 1):]

def _block_diag(u, w, b):
    bsz, t, _ = u.shape
    ub = u.reshape(bsz, t, N_GATE_BLOCKS, GATE_BLOCK)
    return jnp.einsum('btnc,ncd->btnd', ub, w).reshape(bsz, t, D_RNN) + b

def _rglru(u, h0, w_gx, b_gx, w_ga, b_ga, lam):
    uf = u.astype(jnp.float32)
    i_t = jax.nn.sigmoid(_block_diag(u, w_gx, b_gx).astype(jnp.float32))
    r_t = jax.nn.sigmoid(_block_diag(u, w_ga, b_ga).astype(jnp.float32))
    log_a = LRU_C * r_t * jax.nn.log_sigmoid(lam.astype(jnp.float32))
    a = jnp.exp(log_a)
    mult = jnp.sqrt(-jnp.expm1(2.0 * log_a))
    bx = mult * i_t * uf
    bx = bx.at[:, 0].add(a[:, 0] * h0.astype(jnp.float32))

    def combine(l, r):
        return (l[0] * r[0], r[0] * l[1] + r[1])

    _, h = lax.associative_scan(combine, (a, bx), axis=1)
    return h, h[:, -1]

def _layer_a(x, conv_buf, h0, norm_g, w_in, cw, cb, w_gx, b_gx, w_ga, b_ga, lam, w_out):
    u = _rmsnorm(x, norm_g) @ w_in
    xb, gate = jnp.split(u, 2, axis=-1)
    xc, new_buf = _causal_conv(xb, conv_buf, cw, cb)
    h, h_last = _rglru(xc, h0, w_gx, b_gx, w_ga, b_ga, lam)
    y = (h * jax.nn.silu(gate.astype(jnp.float32))).astype(x.dtype) @ w_out
    return x + y, new_buf.astype(conv_buf.dtype), h_last.astype(h0.dtype)

def _shared_kv(x, norm_g, w_kv, k_norm):
    bsz, t, _ = x.shape
    kv = _rmsnorm(x, norm_g) @ w_kv
    k, v = jnp.split(kv, 2, axis=-1)
    k = _rmsnorm(k.reshape(bsz, t, N_KV, HEAD_DIM), k_norm)
    v = v.reshape(bsz, t, N_KV, HEAD_DIM)
    return k, v

def _sink_attention(q, k, v, sink, valid):
    s = jnp.einsum('bnqhgd,bnkhd->bnhgqk', q.astype(jnp.float32), k.astype(jnp.float32))
    s = s * (HEAD_DIM ** -0.5)
    s = jnp.where(valid[None, :, None, None, None, :], s, NEG)
    sk = sink.astype(jnp.float32).reshape(1, 1, N_KV, GROUP, 1, 1)
    m = jnp.maximum(jnp.max(s, axis=-1, keepdims=True), sk)
    p = jnp.exp(s - m)
    denom = jnp.sum(p, axis=-1, keepdims=True) + jnp.exp(sk - m)
    return jnp.einsum('bnhgqk,bnkhd->bnqhgd', p / denom, v.astype(jnp.float32))

def _band_attend(q, k, v, sink):
    bsz, s = q.shape[:2]
    nc = s // CHUNK
    qc = q.reshape(bsz, nc, CHUNK, N_KV, GROUP, HEAD_DIM)
    pad = ((0, 0), (WINDOW, 0), (0, 0), (0, 0))
    kp = jnp.pad(k, pad).reshape(bsz, nc + WIN_CHUNKS, CHUNK, N_KV, HEAD_DIM)
    vp = jnp.pad(v, pad).reshape(bsz, nc + WIN_CHUNKS, CHUNK, N_KV, HEAD_DIM)
    kb = jnp.concatenate([kp[:, j:j + nc] for j in range(WIN_CHUNKS + 1)], axis=2)
    vb = jnp.concatenate([vp[:, j:j + nc] for j in range(WIN_CHUNKS + 1)], axis=2)
    key_pos = (jnp.arange(nc)[:, None] * CHUNK
               + jnp.arange((WIN_CHUNKS + 1) * CHUNK)[None, :] - WINDOW)
    o = _sink_attention(qc, kb, vb, sink, key_pos >= 0)
    return o.reshape(bsz, s, N_HEADS * HEAD_DIM)

def _step_attend(q, k_all, v_all, sink):
    bsz, t = q.shape[:2]
    qc = q.reshape(bsz, 1, t, N_KV, GROUP, HEAD_DIM)
    valid = jnp.ones((1, k_all.shape[1]), dtype=bool)
    o = _sink_attention(qc, k_all[:, None], v_all[:, None], sink, valid)
    return o.reshape(bsz, t, N_HEADS * HEAD_DIM)

def _layer_b(x, k_att, v_att, is_prompt, norm_g, w_in, q_norm, sink, w_out):
    bsz, t, _ = x.shape
    u = _rmsnorm(x, norm_g) @ w_in
    q, gate = jnp.split(u, 2, axis=-1)
    q = _rmsnorm(q.reshape(bsz, t, N_HEADS, HEAD_DIM), q_norm)
    if is_prompt:
        o = _band_attend(q, k_att, v_att, sink)
    else:
        o = _step_attend(q, k_att, v_att, sink)
    y = (o * jax.nn.silu(gate.astype(jnp.float32))).astype(x.dtype) @ w_out
    return x + y

def _trunk(x, conv_state, h_state, k_cache, v_cache, is_prompt, params):
    (norm_a, w_in_a, conv_w, conv_b, w_gate_x, b_gate_x, w_gate_a, b_gate_a, lru_lambda,
     w_out_a, norm_kv, w_kv, k_norm, norm_b, w_in_b, q_norm, sinks, w_out_b) = params
    new_conv, new_h = [], []
    k_att = v_att = k_buf = v_buf = None
    for layer in range(DEPTH):
        if layer < N_A_LAYERS:
            i = layer
            x, cbuf, hl = _layer_a(x, conv_state[i], h_state[i], norm_a[i], w_in_a[i], conv_w[i],
                                   conv_b[i], w_gate_x[i], b_gate_x[i], w_gate_a[i], b_gate_a[i],
                                   lru_lambda[i], w_out_a[i])
            new_conv.append(cbuf)
            new_h.append(hl)
        else:
            if layer == N_A_LAYERS:
                k_new, v_new = _shared_kv(x, norm_kv, w_kv, k_norm)
                if is_prompt:
                    k_att, v_att = k_new, v_new
                else:
                    k_att = jnp.concatenate([k_cache.astype(k_new.dtype), k_new], axis=1)
                    v_att = jnp.concatenate([v_cache.astype(v_new.dtype), v_new], axis=1)
                k_buf, v_buf = k_att[:, -WINDOW:], v_att[:, -WINDOW:]
            j = layer - N_A_LAYERS
            x = _layer_b(x, k_att, v_att, is_prompt, norm_b[j], w_in_b[j], q_norm[j], sinks[j],
                         w_out_b[j])
    return x, jnp.stack(new_conv), jnp.stack(new_h), k_buf, v_buf

def setup_inputs(seed: int = 0) -> dict:
    key = jax.random.key(seed)
    ks = jax.random.split(key, 32)
    f32 = jnp.float32
    nrm = lambda k, shape, scale: jax.random.normal(k, shape, f32) * scale
    u = jax.random.uniform(ks[14], (N_A_LAYERS, D_RNN), f32, 0.9, 0.999)
    return {
        "x_prompt": nrm(ks[0], (BATCH, SEQ, D_MODEL), 1.0),
        "x_sample": nrm(ks[1], (DEC_BATCH, DEC_SEQ, D_MODEL), 1.0),
        "state_conv": nrm(ks[2], (N_A_LAYERS, DEC_BATCH, CONV_W - 1, D_RNN), 1.0),
        "state_rglru": nrm(ks[3], (N_A_LAYERS, DEC_BATCH, D_RNN), 0.5),
        "cache_k_win": nrm(ks[4], (DEC_BATCH, WINDOW, N_KV, HEAD_DIM), 1.0),
        "cache_v_win": nrm(ks[5], (DEC_BATCH, WINDOW, N_KV, HEAD_DIM), 1.0),
        "norm_a": 1.0 + nrm(ks[6], (N_A_LAYERS, D_MODEL), 0.02),
        "w_in_a": nrm(ks[7], (N_A_LAYERS, D_MODEL, 2 * D_RNN), D_MODEL ** -0.5),
        "conv_w": nrm(ks[8], (N_A_LAYERS, CONV_W, D_RNN), CONV_W ** -0.5),
        "conv_b": nrm(ks[9], (N_A_LAYERS, D_RNN), 0.02),
        "w_gate_x": nrm(ks[10], (N_A_LAYERS, N_GATE_BLOCKS, GATE_BLOCK, GATE_BLOCK), GATE_BLOCK ** -0.5),
        "b_gate_x": nrm(ks[11], (N_A_LAYERS, D_RNN), 0.02),
        "w_gate_a": nrm(ks[12], (N_A_LAYERS, N_GATE_BLOCKS, GATE_BLOCK, GATE_BLOCK), GATE_BLOCK ** -0.5),
        "b_gate_a": nrm(ks[13], (N_A_LAYERS, D_RNN), 0.02),
        "lru_lambda": jnp.log(u) - jnp.log1p(-u),
        "w_out_a": nrm(ks[15], (N_A_LAYERS, D_RNN, D_MODEL), D_RNN ** -0.5),
        "norm_kv": 1.0 + nrm(ks[16], (D_MODEL,), 0.02),
        "w_kv": nrm(ks[17], (D_MODEL, 2 * N_KV * HEAD_DIM), D_MODEL ** -0.5),
        "k_norm": 1.0 + nrm(ks[18], (HEAD_DIM,), 0.02),
        "norm_b": 1.0 + nrm(ks[19], (N_B_LAYERS, D_MODEL), 0.02),
        "w_in_b": nrm(ks[20], (N_B_LAYERS, D_MODEL, 2 * N_HEADS * HEAD_DIM), D_MODEL ** -0.5),
        "q_norm": 1.0 + nrm(ks[21], (N_B_LAYERS, HEAD_DIM), 0.02),
        "sinks": nrm(ks[22], (N_B_LAYERS, N_HEADS), 0.5),
        "w_out_b": nrm(ks[23], (N_B_LAYERS, N_HEADS * HEAD_DIM, D_MODEL), (N_HEADS * HEAD_DIM) ** -0.5),
    }

def reference(x_prompt, x_sample, state_conv, state_rglru, cache_k_win, cache_v_win,
              norm_a, w_in_a, conv_w, conv_b, w_gate_x, b_gate_x, w_gate_a, b_gate_a, lru_lambda,
              w_out_a, norm_kv, w_kv, k_norm, norm_b, w_in_b, q_norm, sinks, w_out_b):
    params = (norm_a, w_in_a, conv_w, conv_b, w_gate_x, b_gate_x, w_gate_a, b_gate_a, lru_lambda,
              w_out_a, norm_kv, w_kv, k_norm, norm_b, w_in_b, q_norm, sinks, w_out_b)
    bp = x_prompt.shape[0]
    conv0 = jnp.zeros((N_A_LAYERS, bp, CONV_W - 1, D_RNN), x_prompt.dtype)
    h0 = jnp.zeros((N_A_LAYERS, bp, D_RNN), x_prompt.dtype)
    y_prompt, conv_p, h_p, k_p, v_p = _trunk(x_prompt, conv0, h0, None, None, True, params)
    y_sample, conv_s, h_s, k_s, v_s = _trunk(x_sample, state_conv, state_rglru, cache_k_win,
                                             cache_v_win, False, params)
    return (y_prompt, y_sample, conv_p, h_p, k_p, v_p, conv_s, h_s, k_s, v_s)


_drawn_inputs = setup_inputs


def setup_inputs(seed=0):
    import zlib

    import numpy as np

    out = dict(_drawn_inputs(seed))
    spreads = {}
    factors = {'b_gate_x': 7.186,
     'b_gate_a': 8.0,
     'norm_kv': 2.853,
     'k_norm': 2.835,
     'norm_b': 8.0,
     'q_norm': 8.0,
     'sinks': 8.0}
    for name, (base, spread) in spreads.items():
        noise = np.random.default_rng([zlib.crc32(name.encode()), seed]).standard_normal(out[name].shape)
        drawn = base * np.exp(spread * noise) if base else spread * noise
        out[name] = __import__('jax').numpy.asarray(drawn.astype(out[name].dtype))
    for name, factor in factors.items():
        out[name] = (out[name] * factor).astype(out[name].dtype)
    return out
```

```python
from contextlib import ExitStack

import concourse.bass as bass
from concourse import mybir
from concourse.alu_op_type import AluOpType as ALU

F32 = mybir.dt.float32
F32R = mybir.dt.float32r
ACT = mybir.ActivationFunctionType
AX = mybir.AxisListType

P = 128
D = 1024
NB = D // P
SAMPLE = 64
PROMPT = 2048
TOTAL = SAMPLE + PROMPT
WINDOW = 128
CHUNK = 64
HEAD = 64
CONV = 4
HALO = CONV - 1
EPS = 1e-6
PT = 352
PN = TOTAL // PT
RT = 264
RN = TOTAL // RT
AT = 256
AN = PROMPT // AT
NG = 4
SLOTS_A, SLOTS_B, SLOTS_C = 8, 6, 2
UNITS_IN_A, UNITS_GATE, UNITS_OUT_A, UNITS_KV = 16, 4, 8, 2
U_A1 = 0
U_GATE = U_A1 + UNITS_IN_A
U_OUT_A = U_GATE + UNITS_GATE
U_KV = U_OUT_A + UNITS_OUT_A
U_B1 = U_KV + UNITS_KV
U_OUT_B = U_B1 + 16
UNITS = U_OUT_B + 8


class Parts:
    pass


def need(eng, sem, value):
    if isinstance(value, int) and value <= 0:
        return
    eng.wait_ge(sem, value)


def run_steps(eng, first, end, last, body):
    for s in range(first):
        body(s, s % 2)
    with eng.Fori(0, (end - first) // 2) as i:
        body(i * 2 + first, 0)
        body(i * 2 + (first + 1), 1)
    for s in range(end, last):
        body(s, s % 2)


def known(s, low, high):
    return low <= s <= high if isinstance(s, int) else True


def cols(start, n):
    return bass.ds(start, n)


def build(nc, A):
    stack = ExitStack()
    with stack:
        def sem(name):
            return stack.enter_context(nc.semaphore(name))

        def sems(name, n):
            return [sem(f"{name}{i}") for i in range(n)]

        def tensors(where):
            def sb(name, shape, dt=F32):
                return where.enter_context(nc.sbuf_tensor(name, shape, dt))
            return sb

        sb = tensors(stack)
        w_hi_a = sb("w_hi_a", [P, SLOTS_A, D], F32R)
        w_lo_a = sb("w_lo_a", [P, SLOTS_A, D], F32R)
        raw = sb("w_raw", [P, 2, D])
        ones = sb("ones", [P, P])
        head_ones = sb("head_ones", [P, P])
        ident = sb("ident", [P, P])
        eps = sb("eps", [P, 1])
        vec = sb("vec", [P, 16, NB])
        sink = sb("sink", [P, 8])
        neg_sink = sb("neg_sink", [P, 8])
        kq_scale = sb("kq_scale", [P, 1])
        half_bias = sb("half_bias", [P, 2, NB])
        decay = sb("decay", [P, NB])
        neg_decay = sb("neg_decay", [P, NB])
        lw = sb("lw", [P, 6, NB])
        h_last = sb("h_last", [P, NB])
        h_sample = sb("h_sample", [P, NB])
        halo = sb("halo", [P, NB, HALO])
        halo_sample = sb("halo_sample", [P, NB, HALO])
        banks = [stack.enter_context(nc.psum_tensor(f"bank{i}", [P, 512], F32)) for i in range(4, 8)]
        s_banks = stack.enter_context(nc.psum_tensor("s_banks", [P, 4, 512], F32))
        bank = [s_banks[:, i, :] for i in range(4)] + [b[:, :] for b in banks]
        N_CONST = 3
        G_A, G_KV, G_B, B_X, B_A, LAM, CB, H0, KN, QN = range(10)
        CW = 10

        raw_loaded = sems("raw_loaded", 2)
        w_high = sem("w_high")
        w_split = sem("w_split")
        const_loaded = sem("const_loaded")
        const_made = sem("const_made")
        const_pool = sem("const_pool")
        lw_step = sem("lw_step")
        lw_act = sem("lw_act")
        phase_end = sem("phase_end")
        misc_stored = sem("misc_stored")

        mid = stack.enter_context(ExitStack())
        msb = tensors(mid)
        w_hi_b = msb("w_hi_b", [P, SLOTS_B, D], F32R)
        w_lo_b = msb("w_lo_b", [P, SLOTS_B, D], F32R)

        def slot(k, extra=None):
            if k < SLOTS_A:
                return w_hi_a[:, k, :], w_lo_a[:, k, :]
            if k < SLOTS_A + SLOTS_B:
                return w_hi_b[:, k - SLOTS_A, :], w_lo_b[:, k - SLOTS_A, :]
            return extra[0][:, k - SLOTS_A - SLOTS_B, :], extra[1][:, k - SLOTS_A - SLOTS_B, :]

        def project_memory(tag, heads):
            with ExitStack() as own:
                b = tensors(own)
                m = Parts()
                m.tag, m.heads = tag, heads
                m.banks = [bank[(0 if heads else 4) + i] for i in range(4)]
                m.sum_bank = bank[4 if heads else 0]
                m.extra = (b(f"{tag}_w_hi", [P, SLOTS_C, D], F32R), b(f"{tag}_w_lo", [P, SLOTS_C, D], F32R))
                m.x = b(f"{tag}_x", [P, 4 if heads else NB, PT])
                m.hi = [b(f"{tag}_hi{i}", [P, NB, PT], F32R) for i in range(2)]
                m.lo = [b(f"{tag}_lo{i}", [P, NB, PT], F32R) for i in range(2)]
                m.sq = b(f"{tag}_sq", [P, 1, PT])
                m.acc = b(f"{tag}_acc", [P, 1, PT])
                m.std = b(f"{tag}_std", [P, PT])
                m.out = b(f"{tag}_out", [P, 4, PT])
                if not heads:
                    m.xb = b(f"{tag}_xb", [P, 2, PT + 2 * HALO])
                if heads:
                    m.q = b(f"{tag}_q", [P, 4, PT])
                    m.q2 = b(f"{tag}_q2", [P, 2, PT])
                    m.qstd = b(f"{tag}_qstd", [P, PT])
            m.x_hi = sem(f"{tag}_x_hi")
            m.x_lo = sem(f"{tag}_x_lo")
            m.sq_done = sem(f"{tag}_sq_done")
            m.sq_added = sem(f"{tag}_sq_added")
            m.ms_done = sem(f"{tag}_ms_done")
            m.std_done = sem(f"{tag}_std_done")
            m.rstd_done = sem(f"{tag}_rstd_done")
            m.proj_done = sem(f"{tag}_proj_done")
            m.evacuated = sem(f"{tag}_evacuated")
            m.silu_done = sem(f"{tag}_silu_done")
            m.q2_done = sem(f"{tag}_q2_done")
            m.qms_done = sem(f"{tag}_qms_done")
            m.qstd_done = sem(f"{tag}_qstd_done")
            m.qrec_done = sem(f"{tag}_qrec_done")
            m.q_normed = sem(f"{tag}_q_normed")
            if not heads:
                m.halo_read, m.conv_step, m.conv_done = sem(f"{tag}_halo_read"), sem(f"{tag}_conv_step"), sem(f"{tag}_conv_done")
                m.halo_set = sem(f"{tag}_halo_set")
            m.x_loaded = sems(f"{tag}_x_loaded", m.x.shape[1])
            m.stored = sems(f"{tag}_stored", m.out.shape[1])
            return m

        a1 = project_memory("a1", False)
        a1.first_weights, a1.next_units = True, UNITS_GATE + UNITS_OUT_A + UNITS_KV
        a1.source, a1.dst, a1.unit, a1.gain, a1.phase = A["xT"], (A["xc"], A["sga"]), U_A1, G_A, 0

        with ExitStack() as own:
            b = tensors(own)
            r = Parts()
            r.sg = b("r_sg", [P, 2, 2, RT])
            r.xc = b("r_xc", [P, NG, 2, RT])
            r.xc_hi = b("r_xc_hi", [P, 2, 2, RT], F32R)
            r.xc_lo = b("r_xc_lo", [P, 2, 2, RT], F32R)
            r.ti = b("r_ti", [P, 2, 2, RT])
            r.tr = b("r_tr", [P, 2, 2, RT])
            r.a = b("r_a", [P, 2, 2, RT])
            r.th = b("r_th", [P, 2, 2, RT])
            r.y_hi = [b(f"r_y_hi{i}", [P, NB, RT], F32R) for i in range(2)]
            r.y_lo = [b(f"r_y_lo{i}", [P, NB, RT], F32R) for i in range(2)]
            r.x1 = b("r_x1", [P, 2, RT])
            r.x1_hi = b("r_x1_hi", [P, 2, RT], F32R)
            r.x1_lo = b("r_x1_lo", [P, 2, RT], F32R)
            r.sq = b("r_sq", [P, 2, RT])
            r.acc = b("r_acc", [P, RT])
            r.std = b("r_std", [P, RT])
            r.rstd = b("r_rstd", [P, RT])
            r.k = b("r_k", [P, RT])
            r.v = b("r_v", [P, RT])
            r.k2 = b("r_k2", [P, RT])
        r.xc_loaded, r.sg_loaded = sems("r_xc_loaded", NG), sems("r_sg_loaded", 2)
        r.x_loaded, r.x1_stored = sems("r_x_loaded", 2), sems("r_x1_stored", 2)
        r.xc_high = sem("r_xc_high")
        r.xc_low = sem("r_xc_low")
        r.gates_done = sem("r_gates_done")
        r.gates_read = sem("r_gates_read")
        r.decayed = sem("r_decayed")
        r.a2_done = sem("r_a2_done")
        r.m2_done = sem("r_m2_done")
        r.ix_done = sem("r_ix_done")
        r.mult_done = sem("r_mult_done")
        r.bx_done = sem("r_bx_done")
        r.scan_done = sem("r_scan_done")
        r.h_kept = sem("r_h_kept")
        r.y_done = sem("r_y_done")
        r.y_high = sem("r_y_high")
        r.y_low = sem("r_y_low")
        r.out_done = sem("r_out_done")
        r.resid_done = sem("r_resid_done")
        r.x1_high = sem("r_x1_high")
        r.x1_low = sem("r_x1_low")
        r.sq_done = sem("r_sq_done")
        r.sq_added = sem("r_sq_added")
        r.kv_mm = sem("r_kv_mm")
        r.ms_done = sem("r_ms_done")
        r.std_done = sem("r_std_done")
        r.rstd_done = sem("r_rstd_done")
        r.kv_read = sem("r_kv_read")
        r.k2_done = sem("r_k2_done")
        r.kms_done = sem("r_kms_done")
        r.kstd_done = sem("r_kstd_done")
        r.krec_done = sem("r_krec_done")
        r.k_done = sem("r_k_done")
        r.v_stored = sem("r_v_stored")
        r.k_stored = sem("r_k_stored")

        b1 = project_memory("b1", True)
        b1.first_weights, b1.next_units = False, 8
        b1.source, b1.dst, b1.unit, b1.gain, b1.phase = A["x1"], (A["qn"], A["sgb"]), U_B1, G_B, 2
        mid.close()

        with ExitStack() as own:
            b = tensors(own)
            m = Parts()
            m.q = [b(f"m_q{i}", [P, AT // CHUNK, NB, CHUNK]) for i in range(2)]
            m.sg = [b(f"m_sg{i}", [P, NB, AT]) for i in range(2)]
            m.k = [b(f"m_k{i}", [P, 2, WINDOW + AT]) for i in range(2)]
            m.vt = [b(f"m_vt{i}", [P, WINDOW + AT]) for i in range(2)]
            m.v = [b(f"m_v{i}", [P, 5, P]) for i in range(2)]
            m.y_hi = [b(f"m_y_hi{i}", [P, NB, AT + SAMPLE], F32R) for i in range(2)]
            m.y_lo = [b(f"m_y_lo{i}", [P, NB, AT + SAMPLE], F32R) for i in range(2)]
            m.p = b("m_p", [P, 2, 4, 192])
            m.pt_a = b("m_pt_a", [P, 512])
            m.pt_b = b("m_pt_b", [P, 512])
            m.y = b("m_y", [P, 2, 4, CHUNK])
            m.xres = b("m_xres", [P, 2, AT + SAMPLE])
            m.out = b("m_out", [P, 2, AT + SAMPLE])
            m.nmax = b("m_nmax", [P, 2, 4])
            m.nm = b("m_nm", [P, 2, 4])
            m.sm = b("m_sm", [P, 2, 4])
            m.es = b("m_es", [P, 2, 4])
            m.den = b("m_den", [P, 2, 4])
            m.dsum = b("m_dsum", [P, 2, 4])
            m.rden = b("m_rden", [P, 2, 4])
        m.tile_loaded = sems("m_tile_loaded", 2)
        m.xres_loaded, m.stored = sems("m_xres_loaded", 2), sems("m_stored", 2)
        m.k_scaled = sem("m_k_scaled")
        m.s_done = sem("m_s_done")
        m.max_done = sem("m_max_done")
        m.nm_done = sem("m_nm_done")
        m.sm_done = sem("m_sm_done")
        m.exp_done = sem("m_exp_done")
        m.es_done = sem("m_es_done")
        m.dsum_done = sem("m_dsum_done")
        m.rden_done = sem("m_rden_done")
        m.p_done = sem("m_p_done")
        m.t_done = sem("m_t_done")
        m.pta_done = sem("m_pta_done")
        m.ptb_done = sem("m_ptb_done")
        m.pv_done = sem("m_pv_done")
        m.y_done = sem("m_y_done")
        m.y_high = sem("m_y_high")
        m.y_low = sem("m_y_low")
        m.vt_done = sem("m_vt_done")
        m.va_done = sem("m_va_done")
        m.vb_done = sem("m_vb_done")
        m.out_done = sem("m_out_done")
        m.added = sem("m_added")
        m.p_zero = sem("m_p_zero")
        m.v_zero = sem("m_v_zero")

        three = ((0, 0), (0, 1), (1, 0))

        def project_sync(eng, m):
            src = m.source.rearrange("(b p) t -> p b t", p=P)
            nx = m.x.shape[1]

            def body(s, par):
                for j in range(2 * NB):
                    if known(s, 0, PN - 1) and j < NB:
                        blk = j
                        need(eng, m.x_lo, NB * s + blk + 1 - nx)
                        need(eng, m.sq_done, NB * s + blk + 1 - nx)
                        eng.dma_start(m.x[:, blk % nx, :], src[:, blk, cols(s * PT, PT)])\
                           .then_inc(m.x_loaded[blk % nx], 16)
                    if known(s, 1, PN):
                        t = s - 1
                        if j >= NB:
                            eng.wait_ge(m.silu_done, NB * t + j - NB + 1)
                        elif m.heads:
                            eng.wait_ge(m.q_normed, NB * t + j + 1)
                        else:
                            eng.wait_ge(m.conv_done, NB * t + j + 1)
                        dst = m.dst[j // NB].rearrange("(b p) t -> p b t", p=P)
                        eng.dma_start(dst[:, j % NB, cols(t * PT, PT)], m.out[:, place(j), :])\
                           .then_inc(m.stored[place(j)], 16)

            run_steps(eng, 2, PN, PN + 1, body)
            for stored in m.stored:
                eng.wait_ge(stored, 16 * PN * NB // 2)
            eng.sem_inc(phase_end, 1)

        def project_scalar(eng, m):
            nx = m.x.shape[1]

            def input_block(s, par, blk):
                n = NB * s + blk
                eng.wait_ge(m.x_loaded[blk % nx], 16 * ((NB // nx) * s + blk // nx + 1))
                if blk == 0:
                    need(eng, m.proj_done, 2 * NB * (s - 1))
                nc.scalar.activation(m.hi[par][:, blk, :], m.x[:, blk % nx, :], ACT.Copy,
                                     scale=vec[:, m.gain, blk:blk + 1]).then_inc(m.x_hi, 1)
                need(eng, m.sq_added, n)
                nc.scalar.activation(m.sq[:, 0, :], m.x[:, blk % nx, :], ACT.Square).then_inc(m.sq_done, 1)

            def body(s, par):
                t = s - 1
                if known(s, 1, PN):
                    eng.wait_ge(m.ms_done, t + 1)
                    need(eng, m.evacuated, 2 * NB * t)
                    nc.scalar.activation(m.std[:, :], m.sum_bank[:, 0:PT], ACT.Sqrt, scale=1.0 / D,
                                         bias=eps[:, 0:1]).then_inc(m.std_done, 1)
                for j in range(2 * NB):
                    if known(s, 1, PN):
                        if m.heads and j < NB:
                            eng.wait_ge(m.evacuated, 2 * NB * t + j + 1)
                            need(eng, m.qms_done, NB * t + j - 1)
                            nc.scalar.activation(m.q2[:, j % 2, :], m.q[:, j % 4, :], ACT.Square)\
                              .then_inc(m.q2_done, 1)
                    blk = input_place(s, j)
                    if blk is not None:
                        input_block(s, par, blk)
                    if known(s, 1, PN):
                        if m.heads and 2 <= j < NB + 2:
                            q = j - 2
                            eng.wait_ge(m.qms_done, NB * t + q + 1)
                            need(eng, m.q_normed, NB * t + q)
                            nc.scalar.activation(m.qstd[:, :], bank[5 + q % 2][:, 0:PT], ACT.Sqrt,
                                                 scale=1.0 / HEAD, bias=eps[:, 0:1]).then_inc(m.qstd_done, 1)
                        if j >= NB:
                            eng.wait_ge(m.evacuated, 2 * NB * t + j + 1)
                            nc.scalar.activation(m.out[:, place(j), :], m.out[:, place(j), :], ACT.Silu)\
                              .then_inc(m.silu_done, 1)
                    unit = project_unit(m, s, j)
                    if unit:
                        high_part(eng, *unit)

            eng.wait_ge(const_loaded, 16 * N_CONST)
            eng.wait_ge(const_made, 3)
            need(eng, phase_end, m.phase)
            run_steps(eng, 2, PN, PN + 1, body)

        LW_TERMS = 8
        LW_STEPS = 5 + 2 * LW_TERMS + 4

        def decays(eng):
            eng.wait_ge(lw_act, 2)
            steps = [0]

            def step(op):
                steps[0] += 1
                op.then_inc(lw_step, 1)
                eng.wait_ge(lw_step, steps[0])

            e, z, z2, acc, tmp = (lw[:, k, :] for k in (1, 2, 3, 4, 5))
            step(nc.vector.tensor_scalar(tmp, e, 2.0, None, ALU.add))
            step(nc.vector.reciprocal(tmp, tmp))
            step(nc.vector.tensor_tensor(z, e, tmp, ALU.mult))
            step(nc.vector.tensor_tensor(z2, z, z, ALU.mult))
            step(nc.vector.memset(acc, 1.0 / (2 * LW_TERMS + 1)))
            for k in range(LW_TERMS - 1, -1, -1):
                step(nc.vector.tensor_tensor(acc, acc, z2, ALU.mult))
                step(nc.vector.tensor_scalar(acc, acc, 1.0 / (2 * k + 1), None, ALU.add))
            step(nc.vector.tensor_tensor(acc, acc, z, ALU.mult))
            step(nc.vector.tensor_scalar(tmp, vec[:, LAM, :], -1.0, 0.0, ALU.mult, ALU.max))
            step(nc.vector.scalar_tensor_tensor(out=tmp, in0=acc, scalar=2.0, in1=tmp, op0=ALU.mult, op1=ALU.add))
            nc.vector.tensor_scalar(neg_decay[:, :], tmp, -4.0, None, ALU.mult)
            nc.vector.tensor_scalar(decay[:, :], tmp, 4.0, None, ALU.mult).then_inc(lw_step, 1)

        def project_vector(eng, m):
            nx = m.x.shape[1]

            def input_block(s, par, blk):
                n = NB * s + blk
                eng.wait_ge(m.x_hi, n + 1)
                nc.vector.scalar_tensor_tensor(out=m.lo[par][:, blk, :], in0=m.x[:, blk % nx, :],
                                               scalar=vec[:, m.gain, blk:blk + 1], in1=m.hi[par][:, blk, :].bitcast(F32),
                                               op0=ALU.mult, op1=ALU.subtract).then_inc(m.x_lo, 1)
                eng.wait_ge(m.sq_done, n + 1)
                if blk == 0:
                    need(eng, m.ms_done, s)
                    nc.vector.tensor_copy(m.acc[:, 0, :], m.sq[:, 0, :]).then_inc(m.sq_added, 1)
                else:
                    eng.wait_ge(m.sq_added, n)
                    nc.vector.tensor_tensor(m.acc[:, 0, :], m.acc[:, 0, :], m.sq[:, 0, :], ALU.add)\
                      .then_inc(m.sq_added, 1)

            def norm_head(t, q):
                eng.wait_ge(m.qstd_done, NB * t + q + 1)
                nc.vector.reciprocal(m.qstd[:, :], m.qstd[:, :]).then_inc(m.qrec_done, 1)
                eng.wait_ge(m.qrec_done, NB * t + q + 1)
                need(eng, m.stored[place(q)], stored_before(t, q))
                nc.vector.tensor_tensor(m.out[:, place(q), :], m.q[:, q % 4, :], m.qstd[:, :], ALU.mult)\
                  .then_inc(m.q_normed, 1)

            def continue_input(s, par, j):
                blk = input_place(s, j)
                if blk is not None:
                    input_block(s, par, blk)
                if m.first_weights and isinstance(s, int) and s == PN and j == NB:
                    decays(eng)
                unit = project_unit(m, s, j)
                if unit and unit[0] < VECTOR_UNITS:
                    low_part(eng, nc.vector, unit[0])

            def body(s, par):
                t = s - 1
                if known(s, 1, PN):
                    eng.wait_ge(m.std_done, t + 1)
                    nc.vector.reciprocal(m.std[:, :], m.std[:, :]).then_inc(m.rstd_done, 1)
                for j in range(2 * NB):
                    if known(s, 1, PN):
                        eng.wait_ge(m.rstd_done, t + 1)
                        eng.wait_ge(m.proj_done, 2 * NB * t + j + 1)
                        if m.heads and NB <= j < NB + 3:
                            norm_head(t, j - 3)
                        if j >= NB:
                            need(eng, m.stored[place(j)], stored_before(t, j))
                            dst = m.out[:, place(j), :]
                        elif m.heads:
                            dst = m.q[:, j % 4, :]
                        else:
                            branch(s, t, j)
                            continue_input(s, par, j)
                            continue
                        if m.heads and j < NB:
                            need(eng, m.q_normed, NB * t + j - 3)
                        nc.vector.tensor_tensor(dst, m.banks[j % 4][:, 0:PT], m.std[:, :], ALU.mult)\
                          .then_inc(m.evacuated, 1)
                        if m.heads and 3 <= j < NB:
                            norm_head(t, j - 3)
                    continue_input(s, par, j)

            def branch(s, t, j):
                n, q = NB * t + j, j % 2
                first = isinstance(t, int) and t == 0
                parts = ((0, 0, SAMPLE), (SAMPLE + HALO, SAMPLE, PT - SAMPLE)) if first else ((0, 0, PT),)
                need(eng, m.conv_done, n - 1)
                for w0, o, width in parts:
                    op = nc.vector.tensor_tensor(m.xb[:, q, w0 + HALO:w0 + HALO + width], m.banks[j % 4][:, o:o + width],
                                                 m.std[:, o:o + width], ALU.mult)
                op.then_inc(m.evacuated, 1)
                need(eng, m.halo_set, n - NB + 1)
                nc.vector.tensor_copy(m.xb[:, q, 0:HALO], halo[:, j, :]).then_inc(m.halo_read, 1)
                if first:
                    nc.vector.memset(m.xb[:, q, HALO + SAMPLE:2 * HALO + SAMPLE], 0.0).then_inc(m.halo_read, 1)
                    eng.wait_ge(m.halo_read, 2 * (j + 1))
                else:
                    eng.wait_ge(m.halo_read, NB + n + 1)
                eng.wait_ge(m.evacuated, 2 * NB * t + j + 1)
                need(eng, m.stored[place(j)], stored_before(t, j))
                base = 6 * j if first else 3 * NB + 3 * n
                for tap in range(CONV):
                    if tap:
                        eng.wait_ge(m.conv_step, base + len(parts) * tap)
                    for w0, o, width in parts:
                        x = m.xb[:, q, w0 + tap:w0 + tap + width]
                        out = m.out[:, place(j), o:o + width]
                        if tap == 0:
                            op = nc.vector.tensor_scalar(out, x, vec[:, CW, j:j + 1], vec[:, CB, j:j + 1],
                                                         ALU.mult, ALU.add)
                        else:
                            op = nc.vector.scalar_tensor_tensor(out=out, in0=x, scalar=vec[:, CW + tap, j:j + 1],
                                                                in1=out, op0=ALU.mult, op1=ALU.add)
                        if tap < CONV - 1:
                            op.then_inc(m.conv_step, 1)
                op.then_inc(m.conv_done, 1)
                if first:
                    nc.vector.tensor_copy(halo_sample[:, j, :], m.xb[:, q, SAMPLE:SAMPLE + HALO])
                    end = PT + HALO
                else:
                    end = PT
                nc.vector.tensor_copy(halo[:, j, :], m.xb[:, q, end:end + HALO]).then_inc(m.halo_set, 1)

            need(eng, phase_end, m.phase)
            run_steps(eng, 2, PN, PN + 1, body)

        def project_tensor(eng, m):
            def head_sum(t, q):
                eng.wait_ge(m.q2_done, NB * t + q + 1)
                need(eng, m.qstd_done, NB * t + q - 1)
                nc.tensor.matmul(bank[5 + q % 2][:, 0:PT], head_ones[:, :], m.q2[:, q % 2, :], start=True, stop=True)\
                  .then_inc(m.qms_done, 1)

            def body(s, par):
                if not known(s, 1, PN):
                    return
                t, tp = s - 1, 1 - par
                for j in range(2 * NB):
                    eng.wait_ge(w_split, m.unit + j + 1)
                    need(eng, m.evacuated, 2 * NB * t + j - 3)
                    w = slot(j, m.extra)
                    for n, (kt, (pw, px)) in enumerate((kt, q) for kt in range(NB) for q in three):
                        if j == 0 and n % 3 == 0:
                            eng.wait_ge(m.x_lo, NB * t + kt + 1)
                        x = (m.hi, m.lo)[px][tp]
                        mm = nc.tensor.matmul(m.banks[j % 4][:, 0:PT], w[pw][:, kt * P:(kt + 1) * P], x[:, kt, :],
                                              start=(n == 0), stop=(n == 3 * NB - 1))
                    mm.then_inc(m.proj_done, 1)
                    if j == 0:
                        eng.wait_ge(m.sq_added, NB * (t + 1))
                        need(eng, m.std_done, t)
                        nc.tensor.matmul(m.sum_bank[:, 0:PT], ones[:, :], m.acc[:, 0, :], start=True, stop=True)\
                          .then_inc(m.ms_done, 1)
                    if m.heads and 2 <= j < NB + 2:
                        head_sum(t, j - 2)

            eng.wait_ge(const_made, 5)
            eng.wait_ge(const_pool, 2)
            need(eng, phase_end, m.phase)
            run_steps(eng, 2, PN, PN + 1, body)

        VECTOR_UNITS = 4

        def load_unit(eng, u):
            need(eng, w_split, u - 1)
            eng.dma_start(raw[:, u % 2, :], A["weights"][u, :, :]).then_inc(raw_loaded[u % 2], 16)

        def slot_of(u):
            if u < U_GATE:
                return slot(u - U_A1, a1.extra)
            if u < U_B1:
                return slot(u - U_GATE)
            return slot(u - U_B1, b1.extra) if u < U_OUT_B else slot(u - U_OUT_B)

        def high_part(eng, u, freed=None, count=0):
            eng.wait_ge(raw_loaded[u % 2], 16 * (u // 2 + 1))
            if freed is not None:
                eng.wait_ge(freed, count)
            nc.scalar.activation(slot_of(u)[0], raw[:, u % 2, :], ACT.Copy).then_inc(w_high, 1)

        def low_part(eng, ops, u):
            high, low = slot_of(u)
            eng.wait_ge(w_high, u + 1)
            ops.tensor_tensor(low, raw[:, u % 2, :], high.bitcast(F32), ALU.subtract).then_inc(w_split, 1)

        def low_units(eng, first, end):
            for u in range(first, end):
                if u >= VECTOR_UNITS:
                    low_part(eng, nc.gpsimd, u)
                if u + 2 < UNITS:
                    load_unit(eng, u + 2)

        def place(j):
            return 2 * (j // NB) + j % 2

        def stored_before(t, j):
            return 16 * (NB // 2 * t + j % NB // 2)

        def input_place(s, j):
            blk = j if isinstance(s, int) and s == 0 else j - 3
            return blk if known(s, 0, PN - 1) and 0 <= blk < NB else None

        def project_unit(m, s, j):
            if not isinstance(s, int):
                return None
            if m.first_weights and s == 0 and j in (0, 2, 4, 6, 8):
                return (m.unit + j // 2,)
            if m.first_weights and s == 1 and j + 5 < 2 * NB:
                return (m.unit + 5 + j,)
            if not m.first_weights and s == 0 and j >= SLOTS_A + SLOTS_B:
                return (m.unit + j,)
            if s == PN and 1 <= j <= m.next_units:
                k = j - 1
                return m.unit + 2 * NB + k, m.proj_done, 2 * NB * (PN - 1) + k + 1
            return None

        def recurrent_units(s, g):
            places = {(RN, 0): 0, (RN, 1): 2, (RN, 3): 4, (RN + 1, 0): 6, (RN + 1, 1): 8, (RN + 1, 2): 10,
                      (RN + 1, 3): 12}
            if not isinstance(s, int) or (s, g) not in places:
                return []
            out = []
            for k in (places[s, g], places[s, g] + 1):
                if k < UNITS_GATE:
                    freed, count = r.gates_done, 4 * NG * RN
                elif k < UNITS_GATE + UNITS_OUT_A:
                    freed, count = r.out_done, NB * (RN - 1) + k - UNITS_GATE + 1
                else:
                    freed, count = r.kv_mm, NB * RN
                out.append((U_B1 + k, freed, count))
            return out

        xc_src = A["xc"].rearrange("(b p) t -> p b t", p=P)
        sga_src = A["sga"].rearrange("(b p) t -> p b t", p=P)
        x_src = A["xT"].rearrange("(b p) t -> p b t", p=P)
        x1_dst = A["x1"].rearrange("(b p) t -> p b t", p=P)
        conv0 = A["conv0"].rearrange("(b p) t -> p b t", p=P)

        def back_pair(s, g):
            t, pair, lag = (s - 1, g - 2, 1) if g >= 2 else (s - 2, g + 2, 2)
            return (t, 2 * pair) if known(s, lag, RN - 1 + lag) else None

        def lagged(s, par, g, d):
            if g >= d:
                return (s, par, g - d) if known(s, 0, RN - 1) else None
            return (s - 1, 1 - par, g - d + NG) if known(s, 1, RN) else None

        def recurrent_sync(eng):
            def load_branch(s, g):
                need(eng, r.ix_done, NG * (s - 1) + g + 1)
                eng.dma_start(r.xc[:, g, :, :], xc_src[:, 2 * g:2 * g + 2, cols(s * RT, RT)])\
                   .then_inc(r.xc_loaded[g], 16)

            def load_gate(s, g):
                n, q = NG * s + g, g % 2
                need(eng, r.y_done, n - 1)
                eng.dma_start(r.sg[:, q, :, :], sga_src[:, 2 * g:2 * g + 2, cols(s * RT, RT)])\
                   .then_inc(r.sg_loaded[q], 16)

            def load_x(pair, q):
                t, blk = pair[0], pair[1] + q
                need(eng, r.x1_stored[q], 16 * (NB // 2 * t + blk // 2))
                need(eng, r.sq_done, NB * t + blk - 1)
                need(eng, r.x1_low, NB * t + blk - 1)
                eng.dma_start(r.x1[:, q, :], x_src[:, blk, cols(t * RT, RT)]).then_inc(r.x_loaded[q], 16)

            def store_x1(pair, q):
                t, blk = pair[0], pair[1] + q
                eng.wait_ge(r.resid_done, NB * t + blk + 1)
                eng.dma_start(x1_dst[:, blk, cols(t * RT, RT)], r.x1[:, q, :]).then_inc(r.x1_stored[q], 16)

            def body(s, par):
                for g in range(NG):
                    pair = back_pair(s, g)
                    ahead = back_pair(s, g + 1) if g < NG - 1 else back_pair(s + 1, 0)
                    if g < 2 and known(s, 0, RN - 1):
                        load_branch(s, g + 2)
                    if g >= 2 and known(s, 0, RN - 2):
                        load_branch(s + 1, g - 2)
                    if pair:
                        store_x1(pair, 0)
                    if known(s, 0, RN - 1):
                        load_gate(s, g)
                    if ahead:
                        load_x(ahead, 0)
                    if pair:
                        store_x1(pair, 1)
                    if ahead:
                        load_x(ahead, 1)
                    if known(s, 2, RN + 1) and g == 3:
                        t = s - 2
                        eng.wait_ge(r.kv_read, 2 * (t + 1))
                        eng.dma_start(A["v"][:, cols(t * RT, RT)], r.v[:, :]).then_inc(r.v_stored, 16)
                        eng.wait_ge(r.k_done, t + 1)
                        eng.dma_start(A["k"][:, cols(t * RT, RT)], r.k[:, :]).then_inc(r.k_stored, 16)

            eng.wait_ge(phase_end, 1)
            load_branch(0, 0)
            load_branch(0, 1)
            run_steps(eng, 2, RN - 2, RN + 2, body)
            eng.wait_ge(a1.halo_set, NB * PN)
            for state, name in ((halo_sample, "conv_sample"), (halo, "conv_prompt")):
                eng.dma_start(A[name].rearrange("(b p) t -> p b t", p=P), state[:, :, :]).then_inc(misc_stored, 16)
            eng.wait_ge(r.h_kept, NG * RN)
            eng.dma_start(A["h_prompt"], h_last[:, :]).then_inc(misc_stored, 16)
            eng.dma_start(A["h_sample"], h_sample[:, :]).then_inc(misc_stored, 16)
            eng.wait_ge(misc_stored, 64)
            eng.wait_ge(r.v_stored, 16 * RN)
            eng.wait_ge(r.k_stored, 16 * RN)
            for i in range(2):
                eng.wait_ge(r.x1_stored[i], 16 * RN * NB // 2)
            eng.sem_inc(phase_end, 1)

        def recurrent_vector(eng):
            def high(s, g):
                n, q = NG * s + g, g % 2
                eng.wait_ge(r.xc_loaded[g], 16 * (s + 1))
                need(eng, r.gates_done, 4 * (n - 1))
                nc.vector.tensor_copy(r.xc_hi[:, q, :, :], r.xc[:, g, :, :]).then_inc(r.xc_high, 1)

            def one_minus(s, par, g):
                n, q = NG * s + g, g % 2
                eng.wait_ge(r.a2_done, n + 1)
                nc.vector.scalar_tensor_tensor(out=r.th[:, q, :, :], in0=r.tr[:, q, :, :], scalar=1.0,
                                               in1=r.th[:, q, :, :], op0=ALU.add, op1=ALU.mult).then_inc(r.m2_done, 1)

            def gated_input(s, par, g):
                n, q = NG * s + g, g % 2
                eng.wait_ge(r.gates_read, 4 * n + 4)
                nc.vector.scalar_tensor_tensor(out=r.ti[:, q, :, :], in0=r.ti[:, q, :, :], scalar=1.0,
                                               in1=r.xc[:, g, :, :], op0=ALU.add, op1=ALU.mult).then_inc(r.ix_done, 1)

            def scan(s, par, g):
                n, q = NG * s + g, g % 2
                first = isinstance(s, int) and s == 0
                eng.wait_ge(r.bx_done, n + 1)
                need(eng, r.h_kept, n - NG + 1)
                for blk in range(2):
                    c = 2 * g + blk
                    if first:
                        nc.vector.tensor_tensor_scan(r.th[:, q, blk, 0:SAMPLE], r.a[:, q, blk, 0:SAMPLE],
                                                     r.ti[:, q, blk, 0:SAMPLE], vec[:, H0, c:c + 1],
                                                     ALU.mult, ALU.add)
                        i = nc.vector.tensor_tensor_scan(r.th[:, q, blk, SAMPLE:RT], r.a[:, q, blk, SAMPLE:RT],
                                                         r.ti[:, q, blk, SAMPLE:RT], 0.0, ALU.mult, ALU.add)
                    else:
                        i = nc.vector.tensor_tensor_scan(r.th[:, q, blk, :], r.a[:, q, blk, :], r.ti[:, q, blk, :],
                                                         h_last[:, c:c + 1], ALU.mult, ALU.add)
                    i.then_inc(r.scan_done, 1)
                eng.wait_ge(r.scan_done, 2 * n + 2)
                if first:
                    nc.vector.tensor_copy(h_sample[:, 2 * g:2 * g + 2], r.th[:, q, :, SAMPLE - 1])
                nc.vector.tensor_copy(h_last[:, 2 * g:2 * g + 2], r.th[:, q, :, RT - 1]).then_inc(r.h_kept, 1)

            def y_high(s, par, g):
                n, q = NG * s + g, g % 2
                eng.wait_ge(r.y_done, n + 1)
                need(eng, r.out_done, NB * (s - 1))
                nc.vector.tensor_copy(r.y_hi[par][:, 2 * g:2 * g + 2, :], r.th[:, q, :, :]).then_inc(r.y_high, 1)

            def residual(pair, q):
                t, blk = pair[0], pair[1] + q
                mth = NB * t + blk
                eng.wait_ge(r.out_done, mth + 1)
                eng.wait_ge(r.x_loaded[q], 16 * (NB // 2 * t + blk // 2 + 1))
                nc.vector.tensor_tensor(r.x1[:, q, :], bank[4 + q][:, 0:RT], r.x1[:, q, :], ALU.add)\
                  .then_inc(r.resid_done, 1)
                eng.wait_ge(r.resid_done, mth + 1)
                need(eng, r.kv_mm, mth - 1)
                nc.vector.tensor_scalar(r.x1_hi[:, q, :], r.x1[:, q, :], vec[:, G_KV, blk:blk + 1], None, ALU.mult)\
                  .then_inc(r.x1_high, 1)
                need(eng, r.sq_added, mth - 1)
                nc.vector.tensor_tensor(r.sq[:, q, :], r.x1[:, q, :], r.x1[:, q, :], ALU.mult).then_inc(r.sq_done, 1)
                eng.wait_ge(r.x1_high, mth + 1)
                nc.vector.scalar_tensor_tensor(out=r.x1_lo[:, q, :], in0=r.x1[:, q, :],
                                               scalar=vec[:, G_KV, blk:blk + 1], in1=r.x1_hi[:, q, :].bitcast(F32),
                                               op0=ALU.mult, op1=ALU.subtract).then_inc(r.x1_low, 1)

            def add_square(pair, q):
                t, blk = pair[0], pair[1] + q
                mth = NB * t + blk
                eng.wait_ge(r.sq_done, mth + 1)
                if blk == 0:
                    need(eng, r.ms_done, t)
                    nc.vector.tensor_copy(r.acc[:, :], r.sq[:, q, :]).then_inc(r.sq_added, 1)
                else:
                    eng.wait_ge(r.sq_added, mth)
                    nc.vector.tensor_tensor(r.acc[:, :], r.acc[:, :], r.sq[:, q, :], ALU.add).then_inc(r.sq_added, 1)

            def tail_read(t):
                eng.wait_ge(r.std_done, t + 1)
                need(eng, r.kv_read, 2 * t)
                nc.vector.reciprocal(r.rstd[:, :], r.std[:, :]).then_inc(r.rstd_done, 1)
                eng.wait_ge(r.rstd_done, t + 1)
                eng.wait_ge(r.kv_mm, NB * (t + 1))
                need(eng, r.k_stored, 16 * t)
                nc.vector.tensor_tensor(r.k[:, :], bank[6][:, 0:RT], r.rstd[:, :], ALU.mult).then_inc(r.kv_read, 1)
                need(eng, r.v_stored, 16 * t)
                nc.vector.tensor_tensor(r.v[:, :], bank[7][:, 0:RT], r.rstd[:, :], ALU.mult).then_inc(r.kv_read, 1)
                eng.wait_ge(r.kv_read, 2 * t + 1)
                need(eng, r.kms_done, t)
                nc.vector.tensor_tensor(r.k2[:, :], r.k[:, :], r.k[:, :], ALU.mult).then_inc(r.k2_done, 1)

            def tail_norm(t):
                eng.wait_ge(r.kstd_done, t + 1)
                nc.vector.reciprocal(r.std[:, :], r.std[:, :]).then_inc(r.krec_done, 1)
                eng.wait_ge(r.krec_done, t + 1)
                nc.vector.scalar_tensor_tensor(out=r.k[:, :], in0=r.k[:, :], scalar=vec[:, KN, 0:1], in1=r.std[:, :],
                                               op0=ALU.mult, op1=ALU.mult).then_inc(r.k_done, 1)

            def body(s, par):
                for g in range(NG):
                    one, two, pair = lagged(s, par, g, 1), lagged(s, par, g, 2), back_pair(s, g)
                    if known(s, 0, RN - 1):
                        high(s, g)
                    if one:
                        one_minus(*one)
                    if two:
                        scan(*two)
                    if one:
                        gated_input(*one)
                    if pair:
                        residual(pair, 0)
                    if two:
                        y_high(*two)
                    if known(s, 2, RN + 1) and g == 2:
                        tail_read(s - 2)
                    if known(s, 2, RN + 1) and g == 3:
                        tail_norm(s - 2)
                    if pair:
                        add_square(pair, 0)
                        residual(pair, 1)
                        add_square(pair, 1)

            eng.wait_ge(phase_end, 1)
            run_steps(eng, 2, RN, RN + 2, body)

        def recurrent_scalar(eng):
            def multiplier(s, par, g):
                n, q = NG * s + g, g % 2
                eng.wait_ge(r.m2_done, n + 1)
                nc.scalar.activation(r.th[:, q, :, :], r.th[:, q, :, :], ACT.Sqrt, scale=0.25).then_inc(r.mult_done, 1)

            def gates(s, g):
                n, q = NG * s + g, g % 2
                need(eng, r.scan_done, 2 * (n - 1))
                for mat, dst in enumerate((r.ti, r.tr)):
                    for blk in range(2):
                        c = 2 * g + blk
                        eng.wait_ge(r.gates_done, 4 * n + 2 * mat + blk + 1)
                        nc.scalar.activation(dst[:, q, blk, :], bank[2 * mat + blk][:, 0:RT], ACT.Tanh, scale=0.5,
                                             bias=half_bias[:, mat, c:c + 1]).then_inc(r.gates_read, 1)
                eng.wait_ge(r.gates_read, 4 * n + 4)
                for blk in range(2):
                    c = 2 * g + blk
                    nc.scalar.activation(r.a[:, q, blk, :], r.tr[:, q, blk, :], ACT.Exp, scale=neg_decay[:, c:c + 1],
                                         bias=neg_decay[:, c:c + 1]).then_inc(r.decayed, 1)
                need(eng, r.y_low, n - 1)
                for blk in range(2):
                    c = 2 * g + blk
                    nc.scalar.activation(r.th[:, q, blk, :], r.tr[:, q, blk, :], ACT.Tanh, scale=decay[:, c:c + 1],
                                         bias=decay[:, c:c + 1]).then_inc(r.decayed, 1)
                eng.wait_ge(r.decayed, 4 * n + 4)
                nc.scalar.activation(r.tr[:, q, :, :], r.a[:, q, :, :], ACT.Square).then_inc(r.a2_done, 1)

            def body(s, par):
                for g in range(NG):
                    one, t = lagged(s, par, g, 1), s - 2
                    if one:
                        multiplier(*one)
                    if known(s, 2, RN + 1) and g == 2:
                        eng.wait_ge(r.ms_done, t + 1)
                        need(eng, r.k_done, t)
                        nc.scalar.activation(r.std[:, :], bank[5][:, 0:RT], ACT.Sqrt, scale=1.0 / D,
                                             bias=eps[:, 0:1]).then_inc(r.std_done, 1)
                    if known(s, 2, RN + 1) and g == 3:
                        eng.wait_ge(r.rstd_done, t + 1)
                        eng.wait_ge(r.kms_done, t + 1)
                        nc.scalar.activation(r.std[:, :], bank[5][:, 0:RT], ACT.Sqrt, scale=1.0 / HEAD,
                                             bias=eps[:, 0:1]).then_inc(r.kstd_done, 1)
                    if known(s, 0, RN - 1):
                        gates(s, g)
                    for unit in recurrent_units(s, g):
                        high_part(eng, *unit)

            eng.wait_ge(phase_end, 1)
            run_steps(eng, 2, RN, RN + 2, body)

        def recurrent_gpsimd(eng):
            def low(s, g):
                n, q = NG * s + g, g % 2
                eng.wait_ge(r.xc_high, n + 1)
                need(eng, r.gates_done, 4 * (n - 1))
                nc.gpsimd.tensor_tensor(r.xc_lo[:, q, :, :], r.xc[:, g, :, :],
                                        r.xc_hi[:, q, :, :].bitcast(F32), ALU.subtract).then_inc(r.xc_low, 1)

            def output(s, par, g):
                n, q = NG * s + g, g % 2
                eng.wait_ge(r.h_kept, n + 1)
                eng.wait_ge(r.sg_loaded[q], 16 * (2 * s + g // 2 + 1))
                nc.gpsimd.tensor_tensor(r.th[:, q, :, :], r.th[:, q, :, :], r.sg[:, q, :, :], ALU.mult)\
                  .then_inc(r.y_done, 1)
                eng.wait_ge(r.y_high, n + 1)
                nc.gpsimd.tensor_tensor(r.y_lo[par][:, 2 * g:2 * g + 2, :], r.th[:, q, :, :],
                                        r.y_hi[par][:, 2 * g:2 * g + 2, :].bitcast(F32), ALU.subtract)\
                  .then_inc(r.y_low, 1)

            def scan_input(s, par, g):
                n, q = NG * s + g, g % 2
                eng.wait_ge(r.ix_done, n + 1)
                eng.wait_ge(r.mult_done, n + 1)
                nc.gpsimd.tensor_tensor(r.ti[:, q, :, :], r.ti[:, q, :, :], r.th[:, q, :, :], ALU.mult)\
                  .then_inc(r.bx_done, 1)

            def body(s, par):
                for g in range(NG):
                    one, two = lagged(s, par, g, 1), lagged(s, par, g, 2)
                    if known(s, 0, RN - 1):
                        low(s, g)
                    if two:
                        output(*two)
                    if one:
                        scan_input(*one)

            eng.wait_ge(phase_end, 1)
            run_steps(eng, 2, RN, RN + 1, body)

        def recurrent_tensor(eng):
            def gates(s, g):
                n, q = NG * s + g, g % 2
                eng.wait_ge(w_split, U_GATE + g + 1)
                eng.wait_ge(r.xc_low, n + 1)
                w, x = slot(g), (r.xc_hi, r.xc_lo)
                for mat in range(2):
                    for ob in range(2):
                        need(eng, r.gates_read, 4 * (n - 1) + 2 * mat + ob + 1)
                        for i, (kt, (pw, px)) in enumerate((kt, c) for kt in range(2) for c in three):
                            at = (mat * 2 + kt) * 2 * P + ob * P
                            mm = nc.tensor.matmul(bank[2 * mat + ob][:, 0:RT], w[pw][:, at:at + P],
                                                  x[px][:, q, kt, :], start=(i == 0), stop=(i == 5))
                        mm.then_inc(r.gates_done, 1)

            def kv(t, blk):
                mth = NB * t + blk
                eng.wait_ge(r.x1_low, mth + 1)
                if blk == 0:
                    need(eng, r.kv_read, 2 * t)
                    eng.wait_ge(w_split, U_KV + 2)
                for o in range(2):
                    w = slot(UNITS_GATE + UNITS_OUT_A + o)
                    for i, (pw, px) in enumerate(three):
                        mm = nc.tensor.matmul(bank[6 + o][:, 0:RT], w[pw][:, blk * P:(blk + 1) * P],
                                              (r.x1_hi, r.x1_lo)[px][:, blk % 2, :],
                                              start=(blk == 0 and i == 0), stop=(blk == NB - 1 and i == 2))
                mm.then_inc(r.kv_mm, 1)

            def out(t, tp, blk):
                mth = NB * t + blk
                if blk == 0:
                    eng.wait_ge(r.y_low, NG * (t + 1))
                if blk == 1:
                    need(eng, r.std_done, t)
                if blk == 3:
                    need(eng, r.kstd_done, t)
                eng.wait_ge(w_split, U_OUT_A + blk + 1)
                need(eng, r.resid_done, mth - 1)
                w = slot(UNITS_GATE + blk)
                for i, (kt, (pw, px)) in enumerate((kt, c) for kt in range(NB) for c in three):
                    mm = nc.tensor.matmul(bank[4 + blk % 2][:, 0:RT], w[pw][:, kt * P:(kt + 1) * P],
                                          (r.y_hi, r.y_lo)[px][tp][:, kt, :], start=(i == 0), stop=(i == 3 * NB - 1))
                mm.then_inc(r.out_done, 1)

            def token_sum(t):
                eng.wait_ge(r.sq_added, NB * (t + 1))
                eng.wait_ge(r.resid_done, NB * (t + 1))
                nc.tensor.matmul(bank[5][:, 0:RT], ones[:, :], r.acc[:, :], start=True, stop=True)\
                  .then_inc(r.ms_done, 1)

            def key_sum(t, last):
                eng.wait_ge(r.k2_done, t + 1)
                if not last:
                    eng.wait_ge(r.resid_done, NB * (t + 1) + 2)
                nc.tensor.matmul(bank[5][:, 0:RT], head_ones[:, :], r.k2[:, :], start=True, stop=True)\
                  .then_inc(r.kms_done, 1)

            def body(s, par):
                for g in range(NG):
                    pair, tail = back_pair(s, g), known(s, 2, RN + 1)
                    if pair:
                        tp = 1 - par if g >= 2 else par
                        out(pair[0], tp, pair[1])
                        if g != 2:
                            kv(pair[0], pair[1] - 1)
                    if tail and g == 2:
                        kv(s - 2, NB - 1)
                        token_sum(s - 2)
                    if tail and g == 3:
                        key_sum(s - 2, not known(s, 2, RN))
                    if known(s, 0, RN - 1):
                        gates(s, g)
                    if pair:
                        out(pair[0], tp, pair[1] + 1)
                        kv(pair[0], pair[1])

            eng.wait_ge(phase_end, 1)
            run_steps(eng, 2, RN, RN + 2, body)

        q_src = A["qn"].rearrange("(b p) t -> p b t", p=P)
        sgb_src = A["sgb"].rearrange("(b p) t -> p b t", p=P)
        k_src = A["k"].rearrange("(n d) t -> d n t", d=HEAD)
        k0_src = A["k0"].rearrange("(n d) t -> d n t", d=HEAD)
        y_dst = A["yT"].rearrange("(b p) t -> p b t", p=P)
        LAST = AN + 1

        def unit_of(s, i):
            return i if isinstance(s, int) and s == 0 else 2 + 8 * (s - 1) + i

        def units(s):
            return 2 if isinstance(s, int) and s == 0 else 8

        def lagged_unit(s, par, i):
            if i:
                return s, par, i - 1
            if isinstance(s, int) and s == 0:
                return None
            before = s - 1
            return before, 1 - par, units(before) - 1

        def out_block(s, i):
            if i == 0:
                return (s - 2, 7) if known(s, 3, LAST) else None
            return (s - 1, i - 1) if known(s, 2, LAST - 1) else None

        def attention_sync(eng):
            def tile(s, par):
                if isinstance(s, int) and s == 0:
                    done = m.tile_loaded[0]
                    eng.dma_start(m.q[0][:, 0, :, :], q_src[:, :, 0:SAMPLE]).then_inc(done, 16)
                    eng.dma_start(m.sg[0][:, :, 0:SAMPLE], sgb_src[:, :, 0:SAMPLE]).then_inc(done, 16)
                    for e in range(2):
                        half = m.k[0][e * HEAD:(e + 1) * HEAD, :, :]
                        eng.dma_start(half[:, :, 0:WINDOW], k0_src).then_inc(done, 16)
                        eng.dma_start(half[:, :, WINDOW:WINDOW + SAMPLE], k_src[:, :, 0:SAMPLE]).then_inc(done, 16)
                    eng.dma_start(m.vt[0][:, 0:WINDOW], A["v0"]).then_inc(done, 16)
                    eng.dma_start(m.vt[0][:, WINDOW:WINDOW + SAMPLE], A["v"][:, 0:SAMPLE]).then_inc(done, 16)
                    return
                done = m.tile_loaded[par]
                at = (s - 1) * AT + SAMPLE
                if not (isinstance(s, int) and s == 1):
                    need(eng, m.y_done, unit_of(s - 1, 0) if not isinstance(s, int) else unit_of(s - 1, 0))
                for j in range(AT // CHUNK):
                    eng.dma_start(m.q[par][:, j, :, :], q_src[:, :, cols(at + j * CHUNK, CHUNK)]).then_inc(done, 16)
                eng.dma_start(m.sg[par][:, :, :], sgb_src[:, :, cols(at, AT)]).then_inc(done, 16)
                first = isinstance(s, int) and s == 1
                w0, width = (WINDOW, AT) if first else (0, WINDOW + AT)
                for e in range(2):
                    eng.dma_start(m.k[par][e * HEAD:(e + 1) * HEAD, :, w0:w0 + width],
                                  k_src[:, :, cols(at - WINDOW + w0, width)]).then_inc(done, 16)
                eng.dma_start(m.vt[par][:, w0:w0 + width], A["v"][:, cols(at - WINDOW + w0, width)]).then_inc(done, 16)

            def body(s, par):
                if known(s, 0, AN):
                    tile(s, par)
                for i in range(units(s) if known(s, 0, AN) else 1):
                    ob = out_block(s, i)
                    if ob and known(s, 0, AN):
                        ts, blk = ob
                        load_residual(ts, blk)

            def load_residual(ts, blk):
                nth = NB * (ts - 1) + blk
                need(eng, m.added, nth - 1)
                eng.dma_start(m.xres[:, blk % 2, 0:AT], x1_dst[:, blk, cols((ts - 1) * AT + SAMPLE, AT)])\
                   .then_inc(m.xres_loaded[blk % 2], 16)

            eng.wait_ge(phase_end, 3)
            run_attention(eng, body)
            load_residual(AN - 1, 7)
            for blk in range(NB):
                need(eng, m.added, NB * (AN - 1) + blk - 1)
                eng.dma_start(m.xres[:, blk % 2, 0:AT], x1_dst[:, blk, TOTAL - AT:TOTAL])\
                   .then_inc(m.xres_loaded[blk % 2], 16)
                eng.dma_start(m.xres[:, blk % 2, AT:AT + SAMPLE], x1_dst[:, blk, 0:SAMPLE])\
                   .then_inc(m.xres_loaded[blk % 2], 16)
            for q in range(2):
                eng.wait_ge(m.stored[q], 16 * (4 * (AN - 1) + 8))
            eng.wait_ge(misc_stored, 160)

        def run_attention(eng, body):
            for s in range(4):
                body(s, s % 2)
            with eng.Fori(0, (AN - 4) // 2) as i:
                body(i * 2 + 4, 0)
                body(i * 2 + 5, 1)
            body(AN, 0)

        def loaded(eng, s, par):
            eng.wait_ge(m.tile_loaded[par], s * 64 + (128 if par == 0 else 64))

        def valid(s, i):
            return WINDOW - CHUNK * (i // 2) if isinstance(s, int) and s == 1 and i < 4 else 0

        def attention_tensor(eng):
            def scores(s, par, i):
                u, (j, n) = unit_of(s, i), divmod(i, 2)
                if i == 0:
                    eng.wait_ge(m.k_scaled, s + 1)
                need(eng, m.exp_done, 4 * (u - 1))
                v0 = valid(s, i)
                for e in range(2):
                    rows = slice(e * HEAD, (e + 1) * HEAD)
                    for bp in range(2):
                        blk = 4 * n + 2 * bp
                        mm = nc.tensor.matmul(s_banks[:, 2 * (i % 2) + e, bp * 192 + v0:(bp + 1) * 192],
                                              m.q[par][rows, j, blk:blk + 2, :].rearrange("p b t -> p (b t)"),
                                              m.k[par][rows, n, j * CHUNK + v0:j * CHUNK + 192],
                                              start=True, stop=True, skip_group_check=True)
                mm.then_inc(m.s_done, 1)

            def transpose_p(s, par, i):
                u = unit_of(s, i)
                eng.wait_ge(m.p_done, u + 1)
                need(eng, m.pta_done, u)
                need(eng, m.ptb_done, u)
                if i == 0:
                    eng.wait_ge(m.va_done, s + 1)
                    eng.wait_ge(m.vb_done, s + 1)
                for k in range(4):
                    nc.tensor.transpose(bank[4][:, k * P:(k + 1) * P], m.p[:, i % 2, k, 0:P], ident[:, :])
                for k in range(4):
                    mm = nc.tensor.transpose(bank[5][:, k * P:(k + 1) * P], m.p[:, i % 2, k, CHUNK:192], ident[:, :])
                mm.then_inc(m.t_done, 1)

            def transpose_v(s, par):
                before = unit_of(s, 0)
                need(eng, m.pta_done, before)
                need(eng, m.ptb_done, before)
                loaded(eng, s, par)
                if isinstance(s, int) and s == 1:
                    eng.wait_ge(m.v_zero, 1)
                pairs = 2 if isinstance(s, int) and s == 0 else 5
                for k in range(min(pairs, 4)):
                    nc.tensor.transpose(bank[4][:, k * P:(k + 1) * P], m.vt[par][:, k * CHUNK:k * CHUNK + P], ident[:, :])
                k = pairs - 1
                nc.tensor.transpose(bank[5][:, 0:P], m.vt[par][:, k * CHUNK:k * CHUNK + P], ident[:, :])\
                  .then_inc(m.vt_done, 1)

            def values(s, par, i):
                u, (j, n) = unit_of(s, i), divmod(i, 2)
                eng.wait_ge(m.pta_done, u + 1)
                eng.wait_ge(m.ptb_done, u + 1)
                eng.wait_ge(m.va_done, s + 1)
                eng.wait_ge(m.vb_done, s + 1)
                need(eng, m.y_done, u)
                for e in range(2):
                    out = bank[6][e * HEAD:(e + 1) * HEAD, 0:AT]
                    nc.tensor.matmul(out, m.v[par][:, j, n * HEAD:(n + 1) * HEAD], m.pt_a[:, e * AT:(e + 1) * AT],
                                     start=True, stop=False, skip_group_check=True)
                    mm = nc.tensor.matmul(out, m.v[par][HEAD:P, j + 1, n * HEAD:(n + 1) * HEAD],
                                          m.pt_b[HEAD:P, e * AT:(e + 1) * AT], start=False, stop=True,
                                          skip_group_check=True)
                mm.then_inc(m.pv_done, 1)

            def output(ts, tp, blk, width):
                nth = NB * (ts - 1) + blk
                eng.wait_ge(w_split, U_OUT_B + blk + 1)
                eng.wait_ge(m.y_low, 2 + 8 * ts)
                need(eng, m.added, nth)
                w = slot(blk)
                for n, (kt, (pw, px)) in enumerate((kt, c) for kt in range(NB) for c in three):
                    mm = nc.tensor.matmul(bank[7][:, 0:width], w[pw][:, kt * P:(kt + 1) * P],
                                          (m.y_hi, m.y_lo)[px][tp][:, kt, 0:width], start=(n == 0),
                                          stop=(n == 3 * NB - 1))
                mm.then_inc(m.out_done, 1)

            def body(s, par):
                for i in range(units(s)):
                    scores(s, par, i)
                    lag = lagged_unit(s, par, i)
                    if lag:
                        transpose_p(*lag)
                    ob = out_block(s, i)
                    if ob:
                        output(ob[0], par if i == 0 else 1 - par, ob[1], AT)
                    if lag:
                        values(*lag)
                    if i == 0:
                        transpose_v(s, par)

            eng.wait_ge(phase_end, 3)
            run_attention(eng, body)
            s, par = LAST, LAST % 2
            lag = lagged_unit(s, par, 0)
            transpose_p(*lag)
            output(s - 2, par, 7, AT)
            values(*lag)
            for blk in range(NB):
                output(s - 1, 1 - par, blk, AT + SAMPLE)

        def attention_vector(eng):
            def scale_keys(s, par):
                loaded(eng, s, par)
                w0, w1 = (0, WINDOW + SAMPLE) if isinstance(s, int) and s == 0 else (0, WINDOW + AT)
                if isinstance(s, int) and s == 1:
                    w0 = WINDOW
                nc.vector.tensor_scalar(m.k[par][:, :, w0:w1], m.k[par][:, :, w0:w1], kq_scale[:, 0:1], None,
                                        ALU.mult).then_inc(m.k_scaled, 1)

            def maximum(s, par, i):
                u, q, n = unit_of(s, i), i % 2, i % 2
                v0 = valid(s, i)
                if v0 and i < 2:
                    eng.wait_ge(m.t_done, u - 1)
                    nc.vector.memset(m.p[:, q, :, 0:WINDOW], 0.0).then_inc(m.p_zero, 1)
                eng.wait_ge(m.s_done, u + 1)
                pair = s_banks[:, 2 * q:2 * q + 2, 0:384].rearrange("p e (b k) -> p e b k", b=2)
                nc.vector.tensor_reduce(m.nmax[:, q, :].rearrange("p (e b) -> p e b", e=2), pair[:, :, :, v0:192],
                                        AX.X, ALU.max, negate=True).then_inc(m.max_done, 1)
                eng.wait_ge(m.max_done, u + 1)
                need(eng, m.exp_done, 4 * (u - 1))
                nc.vector.tensor_tensor(m.nm[:, q, :], m.nmax[:, q, :], neg_sink[:, 4 * n:4 * n + 4], ALU.min)\
                  .then_inc(m.nm_done, 1)
                eng.wait_ge(m.nm_done, u + 1)
                need(eng, m.es_done, u - 1)
                nc.vector.tensor_tensor(m.sm[:, q, :], m.nm[:, q, :], sink[:, 4 * n:4 * n + 4], ALU.add)\
                  .then_inc(m.sm_done, 1)

            def normalise(s, par, i):
                u, q = unit_of(s, i), i % 2
                eng.wait_ge(m.exp_done, 4 * u + 4)
                eng.wait_ge(m.es_done, u + 1)
                nc.vector.tensor_tensor(m.dsum[:, q, :], m.den[:, q, :], m.es[:, q, :], ALU.add).then_inc(m.dsum_done, 1)
                eng.wait_ge(m.dsum_done, u + 1)
                nc.vector.reciprocal(m.rden[:, q, :], m.dsum[:, q, :]).then_inc(m.rden_done, 1)
                eng.wait_ge(m.rden_done, u + 1)
                for k in range(4):
                    op = nc.vector.tensor_scalar(m.p[:, q, k, :], m.p[:, q, k, :], m.rden[:, q, k:k + 1], None, ALU.mult)
                op.then_inc(m.p_done, 1)

            def read_pt_b(s, i):
                u = unit_of(s, i)
                eng.wait_ge(m.t_done, u + 1)
                need(eng, m.pv_done, u)
                nc.vector.tensor_copy(m.pt_b[HEAD:P, :], bank[5][HEAD:P, :]).then_inc(m.ptb_done, 1)

            def read_v(s, par):
                pairs = 2 if isinstance(s, int) and s == 0 else 5
                eng.wait_ge(m.vt_done, s + 1)
                nc.vector.tensor_copy(m.v[par][:, pairs - 1, :], bank[5][:, 0:P]).then_inc(m.vb_done, 1)

            def gate(s, par, i):
                u, (j, n), q = unit_of(s, i), divmod(i, 2), i % 2
                eng.wait_ge(m.pv_done, u + 1)
                need(eng, m.y_low, u - 1)
                c0 = j * CHUNK
                nc.vector.tensor_tensor(m.y[:, q, :, :], bank[6][:, 0:AT].rearrange("p (b t) -> p b t", b=4),
                                        m.sg[par][:, 4 * n:4 * n + 4, c0:c0 + CHUNK], ALU.mult).then_inc(m.y_done, 1)
                eng.wait_ge(m.y_done, u + 1)
                dst = y_part(m.y_hi, s, par, i)
                nc.vector.tensor_copy(dst, m.y[:, q, :, :]).then_inc(m.y_high, 1)

            def add(ts, blk, width):
                nth, q = NB * (ts - 1) + blk, blk % 2
                eng.wait_ge(m.out_done, nth + 1)
                eng.wait_ge(m.xres_loaded[q], residual_count(ts, blk))
                each = 2 if isinstance(ts, int) and ts == AN else 1
                need(eng, m.stored[q], 16 * (4 * (ts - 1) + each * (blk // 2)))
                nc.vector.tensor_tensor(m.out[:, q, 0:width], bank[7][:, 0:width], m.xres[:, q, 0:width], ALU.add)\
                  .then_inc(m.added, 1)

            def body(s, par):
                for i in range(units(s)):
                    lag = lagged_unit(s, par, i)
                    if i == 0:
                        scale_keys(s, par)
                    maximum(s, par, i)
                    if lag:
                        read_pt_b(lag[0], lag[2])
                    normalise(s, par, i)
                    ob = out_block(s, i)
                    if ob:
                        add(ob[0], ob[1], AT)
                    if lag:
                        gate(*lag)
                    if i == 0:
                        read_v(s, par)

            eng.wait_ge(phase_end, 3)
            nc.vector.memset(m.vt[1][:, 0:WINDOW], 0.0).then_inc(m.v_zero, 1)
            run_attention(eng, body)
            s, par = LAST, LAST % 2
            lag = lagged_unit(s, par, 0)
            read_pt_b(lag[0], lag[2])
            add(s - 2, 7, AT)
            gate(*lag)
            for blk in range(NB):
                add(s - 1, blk, AT + SAMPLE)

        def y_part(parts, s, par, i):
            j, n = divmod(i, 2)
            if isinstance(s, int) and s == 0:
                return parts[AN % 2][:, 4 * n:4 * n + 4, AT:AT + SAMPLE]
            return parts[par][:, 4 * n:4 * n + 4, j * CHUNK:(j + 1) * CHUNK]

        def residual_count(ts, blk):
            if isinstance(ts, int) and ts == AN:
                return 16 * (4 * (AN - 1) + 2 * (blk // 2 + 1))
            return 16 * (4 * (ts - 1) + blk // 2 + 1)

        def attention_scalar(eng):
            def store(ts, blk, width):
                nth = NB * (ts - 1) + blk
                eng.wait_ge(m.added, nth + 1)
                eng.dma_start(y_dst[:, blk, cols((ts - 1) * AT + SAMPLE, AT)], m.out[:, blk % 2, 0:AT])\
                   .then_inc(m.stored[blk % 2], 16)
                if width > AT:
                    eng.dma_start(y_dst[:, blk, 0:SAMPLE], m.out[:, blk % 2, AT:width]).then_inc(m.stored[blk % 2], 16)

            def exps(s, i):
                u, q = unit_of(s, i), i % 2
                v0 = valid(s, i)
                eng.wait_ge(m.nm_done, u + 1)
                need(eng, m.t_done, u - 1)
                if v0 and i < 2:
                    eng.wait_ge(m.p_zero, i + 1)
                for e in range(2):
                    for bp in range(2):
                        k = 2 * e + bp
                        nc.scalar.activation(m.p[:, q, k, v0:192],
                                             s_banks[:, 2 * q + e, bp * 192 + v0:(bp + 1) * 192], ACT.Exp,
                                             bias=m.nm[:, q, k:k + 1], accum_out=m.den[:, q, k:k + 1])\
                          .then_inc(m.exp_done, 1)
                eng.wait_ge(m.sm_done, u + 1)
                nc.scalar.activation(m.es[:, q, :], m.sm[:, q, :], ACT.Exp).then_inc(m.es_done, 1)

            def read_pt_a(s, i):
                u = unit_of(s, i)
                eng.wait_ge(m.t_done, u + 1)
                need(eng, m.pv_done, u)
                nc.scalar.activation(m.pt_a[:, :], bank[4][:, :], ACT.Copy).then_inc(m.pta_done, 1)

            def read_v(s, par):
                n = 1 if isinstance(s, int) and s == 0 else 4
                eng.wait_ge(m.vt_done, s + 1)
                nc.scalar.activation(m.v[par][:, 0:n, :], bank[4][:, 0:n * P].rearrange("p (a b) -> p a b", a=n),
                                     ACT.Copy).then_inc(m.va_done, 1)

            def body(s, par):
                for i in range(units(s)):
                    lag = lagged_unit(s, par, i)
                    if lag:
                        read_pt_a(lag[0], lag[2])
                    exps(s, i)
                    ob = out_block(s, i)
                    if ob:
                        store(ob[0], ob[1], AT)
                    if i == 0:
                        read_v(s, par)

            eng.wait_ge(phase_end, 3)
            run_attention(eng, body)
            s, par = LAST, LAST % 2
            lag = lagged_unit(s, par, 0)
            read_pt_a(lag[0], lag[2])
            store(s - 2, 7, AT)
            for blk in range(NB):
                store(s - 1, blk, AT + SAMPLE)

        def attention_gpsimd(eng):
            def low(s, par, i):
                u, q = unit_of(s, i), i % 2
                eng.wait_ge(m.y_high, u + 1)
                nc.gpsimd.tensor_tensor(y_part(m.y_lo, s, par, i), m.y[:, q, :, :],
                                        y_part(m.y_hi, s, par, i).bitcast(F32), ALU.subtract).then_inc(m.y_low, 1)

            eng.wait_ge(phase_end, 3)
            run_attention(eng, lambda s, par: [low(s, par, i) for i in range(units(s))])

        block = stack.enter_context(nc.Block())

        @block.sync
        def _(eng):
            nc.disable_value_cache = True
            eng.dma_start(vec[:, :, :], A["vec"]).then_inc(const_loaded, 16)
            eng.dma_start(sink[:, :], A["sinks"]).then_inc(const_loaded, 16)
            eng.dma_start(halo[:, :, :], conv0).then_inc(const_loaded, 16)
            project_sync(eng, a1)
            recurrent_sync(eng)
            eng.dma_start(A["k_prompt"], A["k"][:, TOTAL - WINDOW:TOTAL]).then_inc(misc_stored, 16)
            eng.dma_start(A["v_prompt"], A["v"][:, TOTAL - WINDOW:TOTAL]).then_inc(misc_stored, 16)
            eng.dma_start(A["k_sample"][:, 0:WINDOW - SAMPLE], A["k0"][:, SAMPLE:WINDOW]).then_inc(misc_stored, 16)
            eng.dma_start(A["k_sample"][:, WINDOW - SAMPLE:WINDOW], A["k"][:, 0:SAMPLE]).then_inc(misc_stored, 16)
            eng.dma_start(A["v_sample"][:, 0:WINDOW - SAMPLE], A["v0"][:, SAMPLE:WINDOW]).then_inc(misc_stored, 16)
            eng.dma_start(A["v_sample"][:, WINDOW - SAMPLE:WINDOW], A["v"][:, 0:SAMPLE]).then_inc(misc_stored, 16)
            project_sync(eng, b1)
            attention_sync(eng)
            nc.disable_value_cache = False

        @block.gpsimd
        def _(eng):
            load_unit(eng, 0)
            load_unit(eng, 1)
            nc.gpsimd.memset(ident[:, :], 0.0).then_inc(const_pool, 1)
            eng.wait_ge(const_pool, 1)
            nc.gpsimd.affine_select(out=ident[:, :], in_=ident[:, :], compare_op=ALU.not_equal, fill=1.0, base=0,
                                    pattern=[[-1, P]], channel_multiplier=1).then_inc(const_pool, 1)
            low_units(eng, 0, U_B1)
            recurrent_gpsimd(eng)
            low_units(eng, U_B1, UNITS)
            attention_gpsimd(eng)

        @block.scalar
        def _(eng):
            eng.wait_ge(const_loaded, 16 * N_CONST)
            nc.scalar.activation(lw[:, 0, :], vec[:, LAM, :], ACT.Abs).then_inc(lw_act, 1)
            eng.wait_ge(lw_act, 1)
            nc.scalar.activation(lw[:, 1, :], lw[:, 0, :], ACT.Exp, scale=-1.0).then_inc(lw_act, 1)
            project_scalar(eng, a1)
            eng.wait_ge(lw_step, LW_STEPS)
            recurrent_scalar(eng)
            project_scalar(eng, b1)
            attention_scalar(eng)

        @block.vector
        def _(eng):
            nc.vector.memset(eps[:, :], EPS).then_inc(const_made, 1)
            nc.vector.memset(ones[:, :], 1.0).then_inc(const_made, 1)
            nc.vector.memset(head_ones[:, :], 0.0).then_inc(const_made, 1)
            eng.wait_ge(const_made, 3)
            for e in range(2):
                nc.vector.memset(head_ones[e * HEAD:(e + 1) * HEAD, e * HEAD:(e + 1) * HEAD], 1.0)\
                  .then_inc(const_made, 1)
            eng.wait_ge(const_loaded, 16 * N_CONST)
            nc.vector.tensor_scalar(neg_sink[:, :], sink[:, :], -1.0, None, ALU.mult).then_inc(const_made, 1)
            nc.vector.tensor_scalar(kq_scale[:, :], vec[:, QN, 0:1], HEAD ** -0.5, None, ALU.mult)\
              .then_inc(const_made, 1)
            nc.vector.tensor_scalar(half_bias[:, :, :], vec[:, B_X:B_A + 1, :], 0.5, None, ALU.mult)\
              .then_inc(const_made, 1)
            project_vector(eng, a1)
            recurrent_vector(eng)
            project_vector(eng, b1)
            attention_vector(eng)

        @block.tensor
        def _(eng):
            project_tensor(eng, a1)
            recurrent_tensor(eng)
            project_tensor(eng, b1)
            attention_tensor(eng)


INPUTS = {"xT": (D, TOTAL), "conv0": (D, HALO), "k0": (P, WINDOW), "v0": (P, WINDOW),
          "weights": (UNITS, P, D), "vec": (P, 16, NB), "sinks": (P, 8)}
OUTPUTS = {"yT": (D, TOTAL), "conv_prompt": (D, HALO), "conv_sample": (D, HALO), "h_prompt": (P, NB),
           "h_sample": (P, NB), "k_prompt": (P, WINDOW), "v_prompt": (P, WINDOW), "k_sample": (P, WINDOW),
           "v_sample": (P, WINDOW)}
SCRATCH = {"xc": (D, TOTAL), "sga": (D, TOTAL), "x1": (D, TOTAL), "qn": (D, TOTAL), "sgb": (D, TOTAL),
           "k": (P, TOTAL), "v": (P, TOTAL)}


def layout(inputs):
    import numpy as np
    g = {k: np.asarray(v) for k, v in inputs.items()}

    def columns(w):
        n = w.shape[1] // P
        return w.reshape(NB, P, n, P).transpose(2, 1, 0, 3).reshape(n, P, D)

    gates = np.stack([g["w_gate_x"][0], g["w_gate_a"][0]], 1)
    gates = gates.reshape(NG, 2, 2, P, 2 * P).transpose(0, 3, 1, 2, 4).reshape(NG, P, D)
    weights = np.concatenate([columns(g["w_in_a"][0]), gates, columns(g["w_out_a"][0]), columns(g["w_kv"]),
                              columns(g["w_in_b"][0]), columns(g["w_out_b"][0])], 0)

    def blocks(v):
        return v.reshape(NB, P).T

    def heads(v):
        return np.tile(np.tile(v, 2)[:, None], (1, NB))

    vec = np.stack([blocks(g["norm_a"][0]), blocks(g["norm_kv"]), blocks(g["norm_b"][0]), blocks(g["b_gate_x"][0]),
                    blocks(g["b_gate_a"][0]), blocks(g["lru_lambda"][0]), blocks(g["conv_b"][0]),
                    blocks(g["state_rglru"][0, 0]), heads(g["k_norm"]), heads(g["q_norm"][0])]
                   + [blocks(g["conv_w"][0, j]) for j in range(CONV)] + [blocks(g["norm_a"][0])] * 2, 1)
    sinks = g["sinks"][0].reshape(2, 2, 2, 2).transpose(2, 0, 3, 1).reshape(2, 8)
    return {
        "xT": np.ascontiguousarray(np.concatenate([g["x_sample"][0], g["x_prompt"][0]], 0).T),
        "conv0": np.ascontiguousarray(g["state_conv"][0, 0].T),
        "k0": np.ascontiguousarray(g["cache_k_win"][0].reshape(WINDOW, P).T),
        "v0": np.ascontiguousarray(g["cache_v_win"][0].reshape(WINDOW, P).T),
        "weights": np.ascontiguousarray(weights),
        "vec": np.ascontiguousarray(vec),
        "sinks": np.ascontiguousarray(np.repeat(sinks, HEAD, 0)),
    }


def program(nc):
    aps = {}
    for kind, group in (("ExternalInput", INPUTS), ("ExternalOutput", OUTPUTS), ("Internal", SCRATCH)):
        for name, shape in group.items():
            aps[name] = nc.dram_tensor(f"{name}_dram", shape, F32, kind=kind).ap()
    build(nc, aps)


def kernel(**inputs):
    import numpy as np
    import concourse.bacc as bacc
    from concourse.bass_utils import run_bass_kernel_spmd
    arrays = layout(inputs)
    nc = bacc.Bacc("TRN2", target_bir_lowering=False, num_devices=1)
    program(nc)
    result = run_bass_kernel_spmd(nc, [{f"{k}_dram": v for k, v in arrays.items()}], core_ids=[0]).results[0]
    o = {k: np.asarray(result[f"{k}_dram"]) for k in OUTPUTS}
    y = np.ascontiguousarray(o["yT"].T)

    def rows(a):
        return np.ascontiguousarray(a.T)[None, None]

    def state(a):
        return np.ascontiguousarray(a.T).reshape(1, 1, D)

    def window(a):
        return np.ascontiguousarray(a.T).reshape(1, WINDOW, 2, HEAD)

    return (y[None, SAMPLE:], y[None, :SAMPLE], rows(o["conv_prompt"]), state(o["h_prompt"]),
            window(o["k_prompt"]), window(o["v_prompt"]), rows(o["conv_sample"]), state(o["h_sample"]),
            window(o["k_sample"]), window(o["v_sample"]))
```

```python
from contextlib import ExitStack

import concourse.bass as bass
from concourse import mybir
from concourse.alu_op_type import AluOpType as ALU

F32 = mybir.dt.float32
F32R = mybir.dt.float32r
ACT = mybir.ActivationFunctionType
AX = mybir.AxisListType

P = 128
D = 1024
NB = D // P
SAMPLE = 64
PROMPT = 2048
TOTAL = SAMPLE + PROMPT
WINDOW = 128
CHUNK = 64
HEAD = 64
CONV = 4
HALO = CONV - 1
EPS = 1e-6
PT = 352
PN = TOTAL // PT
RT = 264
RN = TOTAL // RT
AT = 256
AN = PROMPT // AT
NG = 4
SLOTS_A, SLOTS_B, SLOTS_C = 8, 6, 2
UNITS_IN_A, UNITS_GATE, UNITS_KV, UNITS_OUT_A = 16, 4, 2, 8
U_A1 = 0
U_GATE = U_A1 + UNITS_IN_A
U_KV = U_GATE + UNITS_GATE
U_OUT_A = U_KV + UNITS_KV
U_B1 = U_OUT_A + UNITS_OUT_A
U_OUT_B = U_B1 + 16
UNITS = U_OUT_B + 8


class Parts:
    pass


def need(eng, sem, value):
    if isinstance(value, int) and value <= 0:
        return
    eng.wait_ge(sem, value)


def run_steps(eng, first, end, last, body):
    for s in range(first):
        body(s, s % 2)
    with eng.Fori(0, (end - first) // 2) as i:
        body(i * 2 + first, 0)
        body(i * 2 + (first + 1), 1)
    for s in range(end, last):
        body(s, s % 2)


def known(s, low, high):
    return low <= s <= high if isinstance(s, int) else True


def cols(start, n):
    return bass.ds(start, n)


def build(nc, A):
    stack = ExitStack()
    with stack:
        def sem(name):
            return stack.enter_context(nc.semaphore(name))

        def sems(name, n):
            return [sem(f"{name}{i}") for i in range(n)]

        def tensors(where):
            def sb(name, shape, dt=F32):
                return where.enter_context(nc.sbuf_tensor(name, shape, dt))
            return sb

        sb = tensors(stack)
        w_hi_a = sb("w_hi_a", [P, SLOTS_A, D], F32R)
        w_lo_a = sb("w_lo_a", [P, SLOTS_A, D], F32R)
        raw = sb("w_raw", [P, 2, D])
        ones = sb("ones", [P, P])
        head_ones = sb("head_ones", [P, P])
        ident = sb("ident", [P, P])
        eps = sb("eps", [P, 1])
        vec = sb("vec", [P, 16, NB])
        sink = sb("sink", [P, 8])
        neg_sink = sb("neg_sink", [P, 8])
        kq_scale = sb("kq_scale", [P, 1])
        half_bias = sb("half_bias", [P, 2, NB])
        decay = sb("decay", [P, NB])
        neg_decay = sb("neg_decay", [P, NB])
        lw = sb("lw", [P, 6, NB])
        h_last = sb("h_last", [P, NB])
        h_sample = sb("h_sample", [P, NB])
        halo = sb("halo", [P, NB, HALO])
        halo_sample = sb("halo_sample", [P, NB, HALO])
        banks = [stack.enter_context(nc.psum_tensor(f"bank{i}", [P, 512], F32)) for i in range(4, 8)]
        s_banks = stack.enter_context(nc.psum_tensor("s_banks", [P, 4, 512], F32))
        bank = [s_banks[:, i, :] for i in range(4)] + [b[:, :] for b in banks]
        N_CONST = 3
        G_A, G_KV, G_B, B_X, B_A, LAM, CB, H0, KN, QN = range(10)
        CW = 10

        raw_loaded = sems("raw_loaded", 2)
        w_high = sem("w_high")
        w_split = sem("w_split")
        const_loaded = sem("const_loaded")
        const_made = sem("const_made")
        const_pool = sem("const_pool")
        lw_step = sem("lw_step")
        lw_act = sem("lw_act")
        recurrent_stored = sem("recurrent_stored")
        misc_stored = sem("misc_stored")

        mid = stack.enter_context(ExitStack())
        msb = tensors(mid)
        w_hi_b = msb("w_hi_b", [P, SLOTS_B, D], F32R)
        w_lo_b = msb("w_lo_b", [P, SLOTS_B, D], F32R)

        def slot(k, extra=None):
            if k < SLOTS_A:
                return w_hi_a[:, k, :], w_lo_a[:, k, :]
            if k < SLOTS_A + SLOTS_B:
                return w_hi_b[:, k - SLOTS_A, :], w_lo_b[:, k - SLOTS_A, :]
            return extra[0][:, k - SLOTS_A - SLOTS_B, :], extra[1][:, k - SLOTS_A - SLOTS_B, :]

        def project_memory(tag, heads):
            with ExitStack() as own:
                b = tensors(own)
                m = Parts()
                m.heads = heads
                m.banks = [bank[(0 if heads else 4) + i] for i in range(4)]
                m.sum_bank = bank[4 if heads else 0]
                hi0, lo0 = b(f"{tag}_hi0", [P, NB, PT], F32R), b(f"{tag}_lo0", [P, NB, PT], F32R)
                m.x = b(f"{tag}_x", [P, 4 if heads else NB, PT])
                if heads:
                    m.sq, m.acc, m.std = b(f"{tag}_sq", [P, 1, PT]), b(f"{tag}_acc", [P, 1, PT]), b(f"{tag}_std", [P, PT])
                m.extra = (b(f"{tag}_w_hi", [P, SLOTS_C, D], F32R), b(f"{tag}_w_lo", [P, SLOTS_C, D], F32R))
                m.hi = [hi0, b(f"{tag}_hi1", [P, NB, PT], F32R)]
                m.lo = [lo0, b(f"{tag}_lo1", [P, NB, PT], F32R)]
                if heads:
                    m.q = b(f"{tag}_q", [P, 4, PT])
                    m.q2 = b(f"{tag}_q2", [P, 2, PT])
                    m.qstd = b(f"{tag}_qstd", [P, PT])
                else:
                    m.std = b(f"{tag}_std", [P, PT])
                m.out = b(f"{tag}_out", [P, 4, PT])
                if not heads:
                    m.xb = b(f"{tag}_xb", [P, 2, PT + 2 * HALO])
                    m.sq, m.acc = b(f"{tag}_sq", [P, 1, PT]), b(f"{tag}_acc", [P, 1, PT])
            m.x_hi = sem(f"{tag}_x_hi")
            m.x_lo = sem(f"{tag}_x_lo")
            m.sq_done = sem(f"{tag}_sq_done")
            m.sq_added = sem(f"{tag}_sq_added")
            m.ms_done = sem(f"{tag}_ms_done")
            m.std_done = sem(f"{tag}_std_done")
            m.rstd_done = sem(f"{tag}_rstd_done")
            m.proj_done = sem(f"{tag}_proj_done")
            m.evacuated = sem(f"{tag}_evacuated")
            m.silu_done = sem(f"{tag}_silu_done")
            m.q2_done = sem(f"{tag}_q2_done")
            m.qms_done = sem(f"{tag}_qms_done")
            m.qstd_done = sem(f"{tag}_qstd_done")
            m.qrec_done = sem(f"{tag}_qrec_done")
            m.q_normed = sem(f"{tag}_q_normed")
            if not heads:
                m.halo_read, m.conv_step, m.conv_done = sem(f"{tag}_halo_read"), sem(f"{tag}_conv_step"), sem(f"{tag}_conv_done")
                m.halo_set = sem(f"{tag}_halo_set")
            m.x_loaded = sems(f"{tag}_x_loaded", m.x.shape[1])
            m.stored = sems(f"{tag}_stored", m.out.shape[1])
            return m

        a1 = project_memory("a1", False)
        a1.first_weights, a1.next_units = True, 11
        a1.source, a1.dst, a1.unit, a1.gain = A["xT"], (A["xc"], A["sga"]), U_A1, G_A

        with ExitStack() as own:
            b = tensors(own)
            r = Parts()
            r.xc = b("r_xc", [P, NG, 2, RT])
            r.xc_hi = b("r_xc_hi", [P, 2, 2, RT], F32R)
            r.xc_lo = b("r_xc_lo", [P, 2, 2, RT], F32R)
            r.ti = b("r_ti", [P, 2, 2, RT])
            r.tr = b("r_tr", [P, 2, 2, RT])
            r.a = b("r_a", [P, 2, 2, RT])
            r.th = b("r_th", [P, 2, 2, RT])
            r.y_hi = [b(f"r_y_hi{i}", [P, NB, RT], F32R) for i in range(2)]
            r.y_lo = [b(f"r_y_lo{i}", [P, NB, RT], F32R) for i in range(2)]
            r.k = b("r_k", [P, RT])
            r.v = b("r_v", [P, RT])
            r.std = b("r_std", [P, RT])
            r.rstd = b("r_rstd", [P, RT])
            r.acc = b("r_acc", [P, RT])
            r.k2 = b("r_k2", [P, RT])
            r.x1 = b("r_x1", [P, 2, RT])
            r.x1_hi = b("r_x1_hi", [P, 2, RT], F32R)
            r.x1_lo = b("r_x1_lo", [P, 2, RT], F32R)
            r.sq = b("r_sq", [P, 2, RT])
            r.sg = b("r_sg", [P, 2, 2, RT])
        r.xc_loaded, r.sg_loaded = sems("r_xc_loaded", NG), sems("r_sg_loaded", 2)
        r.x_loaded, r.x1_stored = sems("r_x_loaded", 2), sems("r_x1_stored", 2)
        r.xc_high = sem("r_xc_high")
        r.xc_low = sem("r_xc_low")
        r.gates_done = sem("r_gates_done")
        r.gates_read = sem("r_gates_read")
        r.decayed = sem("r_decayed")
        r.a2_done = sem("r_a2_done")
        r.m2_done = sem("r_m2_done")
        r.ix_done = sem("r_ix_done")
        r.mult_done = sem("r_mult_done")
        r.bx_done = sem("r_bx_done")
        r.scan_done = sem("r_scan_done")
        r.h_kept = sem("r_h_kept")
        r.y_done = sem("r_y_done")
        r.y_high = sem("r_y_high")
        r.y_low = sem("r_y_low")
        r.out_done = sem("r_out_done")
        r.resid_done = sem("r_resid_done")
        r.x1_high = sem("r_x1_high")
        r.x1_low = sem("r_x1_low")
        r.sq_done = sem("r_sq_done")
        r.sq_added = sem("r_sq_added")
        r.kv_mm = sem("r_kv_mm")
        r.ms_done = sem("r_ms_done")
        r.std_done = sem("r_std_done")
        r.rstd_done = sem("r_rstd_done")
        r.kv_read = sem("r_kv_read")
        r.k2_done = sem("r_k2_done")
        r.kms_done = sem("r_kms_done")
        r.kstd_done = sem("r_kstd_done")
        r.krec_done = sem("r_krec_done")
        r.k_done = sem("r_k_done")
        r.v_stored = sem("r_v_stored")
        r.k_stored = sem("r_k_stored")
        r.x1_free = sem("r_x1_free")

        b1 = project_memory("b1", True)
        b1.first_weights, b1.next_units = False, 8
        b1.source, b1.dst, b1.unit, b1.gain = A["x1"], (A["qn"], A["sgb"]), U_B1, G_B
        mid.close()

        with ExitStack() as own:
            b = tensors(own)
            m = Parts()
            m.y_hi = [b(f"m_y_hi{i}", [P, NB, AT + SAMPLE], F32R) for i in range(2)]
            m.y_lo = [b(f"m_y_lo{i}", [P, NB, AT + SAMPLE], F32R) for i in range(2)]
            m.xres = b("m_xres", [P, 2, AT + SAMPLE])
            m.out = b("m_out", [P, 2, AT + SAMPLE])
            m.pt_a = b("m_pt_a", [P, 512])
            m.nmax = b("m_nmax", [P, 2, 4])
            m.nm = b("m_nm", [P, 2, 4])
            m.sm = b("m_sm", [P, 2, 4])
            m.es = b("m_es", [P, 2, 4])
            m.den = b("m_den", [P, 2, 4])
            m.dsum = b("m_dsum", [P, 2, 4])
            m.rden = b("m_rden", [P, 2, 4])
            used = (4 * NB + 4) * (AT + SAMPLE) + 512 + 7 * 8
            b("m_gap", [P, 2 * SLOTS_B * D - used])
            m.q = [b(f"m_q{i}", [P, AT // CHUNK, NB, CHUNK]) for i in range(2)]
            m.k = [b(f"m_k{i}", [P, 2, WINDOW + AT]) for i in range(2)]
            m.vt = [b(f"m_vt{i}", [P, WINDOW + AT]) for i in range(2)]
            m.v = [b(f"m_v{i}", [P, 5, P]) for i in range(2)]
            m.p = b("m_p", [P, 2, 4, 192])
            m.sg = [b(f"m_sg{i}", [P, NB, AT]) for i in range(2)]
            m.pt_b = b("m_pt_b", [P, 512])
            m.y = b("m_y", [P, 2, 4, CHUNK])
        m.sg_loaded = sems("m_sg_loaded", 2)
        m.tile_loaded = sems("m_tile_loaded", 2)
        m.xres_loaded, m.stored = sems("m_xres_loaded", 2), sems("m_stored", 2)
        m.k_scaled = sem("m_k_scaled")
        m.s_done = sem("m_s_done")
        m.max_done = sem("m_max_done")
        m.nm_done = sem("m_nm_done")
        m.sm_done = sem("m_sm_done")
        m.exp_done = sem("m_exp_done")
        m.es_done = sem("m_es_done")
        m.dsum_done = sem("m_dsum_done")
        m.rden_done = sem("m_rden_done")
        m.p_done = sem("m_p_done")
        m.t_done = sem("m_t_done")
        m.pta_done = sem("m_pta_done")
        m.ptb_done = sem("m_ptb_done")
        m.pv_done = sem("m_pv_done")
        m.y_done = sem("m_y_done")
        m.y_high = sem("m_y_high")
        m.y_low = sem("m_y_low")
        m.vt_done = sem("m_vt_done")
        m.va_done = sem("m_va_done")
        m.vb_done = sem("m_vb_done")
        m.out_done = sem("m_out_done")
        m.added = sem("m_added")
        m.p_zero = sem("m_p_zero")
        m.v_zero = sem("m_v_zero")

        three = ((0, 0), (0, 1), (1, 0))

        def nothing(s, j):
            pass

        def load_input(eng, m, s, blk):
            nx = m.x.shape[1]
            need(eng, m.x_lo, NB * s + blk + 1 - nx)
            need(eng, m.sq_done, NB * s + blk + 1 - nx)
            eng.dma_start(m.x[:, blk % nx, :], m.source.rearrange("(b p) t -> p b t", p=P)[:, blk, cols(s * PT, PT)])\
               .then_inc(m.x_loaded[blk % nx], 16)

        def high_input(eng, m, s, par, blk):
            nx, n = m.x.shape[1], NB * s + blk
            eng.wait_ge(m.x_loaded[blk % nx], 16 * ((NB // nx) * s + blk // nx + 1))
            if blk == 0:
                need(eng, m.proj_done, 2 * NB * (s - 1))
            nc.scalar.activation(m.hi[par][:, blk, :], m.x[:, blk % nx, :], ACT.Copy,
                                 scale=vec[:, m.gain, blk:blk + 1]).then_inc(m.x_hi, 1)
            need(eng, m.sq_added, n)
            nc.scalar.activation(m.sq[:, 0, :], m.x[:, blk % nx, :], ACT.Square).then_inc(m.sq_done, 1)

        def low_input(eng, m, s, par, blk):
            nx, n = m.x.shape[1], NB * s + blk
            eng.wait_ge(m.x_hi, n + 1)
            nc.vector.scalar_tensor_tensor(out=m.lo[par][:, blk, :], in0=m.x[:, blk % nx, :],
                                           scalar=vec[:, m.gain, blk:blk + 1], in1=m.hi[par][:, blk, :].bitcast(F32),
                                           op0=ALU.mult, op1=ALU.subtract).then_inc(m.x_lo, 1)
            eng.wait_ge(m.sq_done, n + 1)
            if blk == 0:
                need(eng, m.ms_done, s)
                nc.vector.tensor_copy(m.acc[:, 0, :], m.sq[:, 0, :]).then_inc(m.sq_added, 1)
            else:
                eng.wait_ge(m.sq_added, n)
                nc.vector.tensor_tensor(m.acc[:, 0, :], m.acc[:, 0, :], m.sq[:, 0, :], ALU.add)\
                  .then_inc(m.sq_added, 1)

        def run_project(eng, m, body):
            if m.first_weights:
                body(0, 0)
            body(1, 1)
            with eng.Fori(0, (PN - 2) // 2) as i:
                body(i * 2 + 2, 0)
                body(i * 2 + 3, 1)
            body(PN, PN % 2)

        def project_sync(eng, m, starts):
            def body(s, par):
                for j in range(2 * NB):
                    if isinstance(s, int) and s == PN and j in starts:
                        starts[j]()
                    if known(s, 0, PN - 1) and j < NB:
                        load_input(eng, m, s, j)
                    if known(s, 1, PN):
                        t = s - 1
                        if j >= NB:
                            eng.wait_ge(m.silu_done, NB * t + j - NB + 1)
                        elif m.heads:
                            eng.wait_ge(m.q_normed, NB * t + j + 1)
                        else:
                            eng.wait_ge(m.conv_done, NB * t + j + 1)
                        dst = m.dst[j // NB].rearrange("(b p) t -> p b t", p=P)
                        eng.dma_start(dst[:, j % NB, cols(t * PT, PT)], m.out[:, place(j), :])\
                           .then_inc(m.stored[place(j)], 16)

            run_project(eng, m, body)
            for stored in m.stored:
                eng.wait_ge(stored, 16 * PN * NB // 2)

        def project_scalar(eng, m, after):
            def body(s, par):
                t = s - 1
                if known(s, 1, PN):
                    eng.wait_ge(m.ms_done, t + 1)
                    need(eng, m.evacuated, 2 * NB * t)
                    nc.scalar.activation(m.std[:, :], m.sum_bank[:, 0:PT], ACT.Sqrt, scale=1.0 / D,
                                         bias=eps[:, 0:1]).then_inc(m.std_done, 1)
                for j in range(2 * NB):
                    if known(s, 1, PN):
                        if m.heads and j < NB:
                            eng.wait_ge(m.evacuated, 2 * NB * t + j + 1)
                            need(eng, m.qms_done, NB * t + j - 1)
                            nc.scalar.activation(m.q2[:, j % 2, :], m.q[:, j % 4, :], ACT.Square)\
                              .then_inc(m.q2_done, 1)
                    blk = input_place(s, j)
                    if blk is not None:
                        if m.heads and blk == 0 and isinstance(s, int) and s == 1:
                            eng.wait_ge(recurrent_stored, 1)
                        high_input(eng, m, s, par, blk)
                    if known(s, 1, PN):
                        if m.heads and 2 <= j < NB + 2:
                            q = j - 2
                            eng.wait_ge(m.qms_done, NB * t + q + 1)
                            need(eng, m.q_normed, NB * t + q)
                            nc.scalar.activation(m.qstd[:, :], bank[5 + q % 2][:, 0:PT], ACT.Sqrt,
                                                 scale=1.0 / HEAD, bias=eps[:, 0:1]).then_inc(m.qstd_done, 1)
                        if j >= NB:
                            eng.wait_ge(m.evacuated, 2 * NB * t + j + 1)
                            nc.scalar.activation(m.out[:, place(j), :], m.out[:, place(j), :], ACT.Silu)\
                              .then_inc(m.silu_done, 1)
                    unit = project_unit(m, s, j)
                    if unit:
                        high_part(eng, *unit)
                    after(s, j)

            run_project(eng, m, body)

        LW_TERMS = 8
        LW_STEPS = 5 + 2 * LW_TERMS + 4

        def decays(eng):
            eng.wait_ge(lw_act, 2)
            steps = [0]

            def step(op):
                steps[0] += 1
                op.then_inc(lw_step, 1)
                eng.wait_ge(lw_step, steps[0])

            e, z, z2, acc, tmp = (lw[:, k, :] for k in (1, 2, 3, 4, 5))
            step(nc.vector.tensor_scalar(tmp, e, 2.0, None, ALU.add))
            step(nc.vector.reciprocal(tmp, tmp))
            step(nc.vector.tensor_tensor(z, e, tmp, ALU.mult))
            step(nc.vector.tensor_tensor(z2, z, z, ALU.mult))
            step(nc.vector.memset(acc, 1.0 / (2 * LW_TERMS + 1)))
            for k in range(LW_TERMS - 1, -1, -1):
                step(nc.vector.tensor_tensor(acc, acc, z2, ALU.mult))
                step(nc.vector.tensor_scalar(acc, acc, 1.0 / (2 * k + 1), None, ALU.add))
            step(nc.vector.tensor_tensor(acc, acc, z, ALU.mult))
            step(nc.vector.tensor_scalar(tmp, vec[:, LAM, :], -1.0, 0.0, ALU.mult, ALU.max))
            step(nc.vector.scalar_tensor_tensor(out=tmp, in0=acc, scalar=2.0, in1=tmp, op0=ALU.mult, op1=ALU.add))
            nc.vector.tensor_scalar(neg_decay[:, :], tmp, -4.0, None, ALU.mult)
            nc.vector.tensor_scalar(decay[:, :], tmp, 4.0, None, ALU.mult).then_inc(lw_step, 1)

        def project_vector(eng, m, after):
            def norm_head(t, q):
                eng.wait_ge(m.qstd_done, NB * t + q + 1)
                nc.vector.reciprocal(m.qstd[:, :], m.qstd[:, :]).then_inc(m.qrec_done, 1)
                eng.wait_ge(m.qrec_done, NB * t + q + 1)
                need(eng, m.stored[place(q)], stored_before(t, q))
                nc.vector.tensor_tensor(m.out[:, place(q), :], m.q[:, q % 4, :], m.qstd[:, :], ALU.mult)\
                  .then_inc(m.q_normed, 1)

            def continue_input(s, par, j):
                blk = input_place(s, j)
                if blk is not None:
                    if m.heads and blk == 0 and isinstance(s, int) and s == 1:
                        eng.wait_ge(recurrent_stored, 1)
                    low_input(eng, m, s, par, blk)
                unit = project_unit(m, s, j)
                if unit and unit[0] < VECTOR_UNITS:
                    low_part(eng, nc.vector, unit[0])
                after(s, j)

            def body(s, par):
                t = s - 1
                if known(s, 1, PN):
                    eng.wait_ge(m.std_done, t + 1)
                    nc.vector.reciprocal(m.std[:, :], m.std[:, :]).then_inc(m.rstd_done, 1)
                for j in range(2 * NB):
                    if known(s, 1, PN):
                        eng.wait_ge(m.rstd_done, t + 1)
                        eng.wait_ge(m.proj_done, 2 * NB * t + j + 1)
                        if m.heads and NB <= j < NB + 3:
                            norm_head(t, j - 3)
                        if j >= NB:
                            need(eng, m.stored[place(j)], stored_before(t, j))
                            dst = m.out[:, place(j), :]
                        elif m.heads:
                            dst = m.q[:, j % 4, :]
                        else:
                            branch(s, t, j)
                            continue_input(s, par, j)
                            continue
                        if m.heads and j < NB:
                            need(eng, m.q_normed, NB * t + j - 3)
                        nc.vector.tensor_tensor(dst, m.banks[j % 4][:, 0:PT], m.std[:, :], ALU.mult)\
                          .then_inc(m.evacuated, 1)
                        if m.heads and 3 <= j < NB:
                            norm_head(t, j - 3)
                    continue_input(s, par, j)

            def branch(s, t, j):
                n, q = NB * t + j, j % 2
                first = isinstance(t, int) and t == 0
                parts = ((0, 0, SAMPLE), (SAMPLE + HALO, SAMPLE, PT - SAMPLE)) if first else ((0, 0, PT),)
                need(eng, m.conv_done, n - 1)
                for w0, o, width in parts:
                    op = nc.vector.tensor_tensor(m.xb[:, q, w0 + HALO:w0 + HALO + width], m.banks[j % 4][:, o:o + width],
                                                 m.std[:, o:o + width], ALU.mult)
                op.then_inc(m.evacuated, 1)
                need(eng, m.halo_set, n - NB + 1)
                nc.vector.tensor_copy(m.xb[:, q, 0:HALO], halo[:, j, :]).then_inc(m.halo_read, 1)
                if first:
                    nc.vector.memset(m.xb[:, q, HALO + SAMPLE:2 * HALO + SAMPLE], 0.0).then_inc(m.halo_read, 1)
                    eng.wait_ge(m.halo_read, 2 * (j + 1))
                else:
                    eng.wait_ge(m.halo_read, NB + n + 1)
                eng.wait_ge(m.evacuated, 2 * NB * t + j + 1)
                need(eng, m.stored[place(j)], stored_before(t, j))
                base = 6 * j if first else 3 * NB + 3 * n
                for tap in range(CONV):
                    if tap:
                        eng.wait_ge(m.conv_step, base + len(parts) * tap)
                    for w0, o, width in parts:
                        x = m.xb[:, q, w0 + tap:w0 + tap + width]
                        out = m.out[:, place(j), o:o + width]
                        if tap == 0:
                            op = nc.vector.tensor_scalar(out, x, vec[:, CW, j:j + 1], vec[:, CB, j:j + 1],
                                                         ALU.mult, ALU.add)
                        else:
                            op = nc.vector.scalar_tensor_tensor(out=out, in0=x, scalar=vec[:, CW + tap, j:j + 1],
                                                                in1=out, op0=ALU.mult, op1=ALU.add)
                        if tap < CONV - 1:
                            op.then_inc(m.conv_step, 1)
                op.then_inc(m.conv_done, 1)
                if first:
                    nc.vector.tensor_copy(halo_sample[:, j, :], m.xb[:, q, SAMPLE:SAMPLE + HALO])
                    end = PT + HALO
                else:
                    end = PT
                nc.vector.tensor_copy(halo[:, j, :], m.xb[:, q, end:end + HALO]).then_inc(m.halo_set, 1)

            run_project(eng, m, body)

        def project_tensor(eng, m, after):
            def head_sum(t, q):
                eng.wait_ge(m.q2_done, NB * t + q + 1)
                need(eng, m.qstd_done, NB * t + q - 1)
                nc.tensor.matmul(bank[5 + q % 2][:, 0:PT], head_ones[:, :], m.q2[:, q % 2, :], start=True, stop=True)\
                  .then_inc(m.qms_done, 1)

            def body(s, par):
                if not known(s, 1, PN):
                    return
                t, tp = s - 1, 1 - par
                for j in range(2 * NB):
                    eng.wait_ge(w_split, m.unit + j + 1)
                    need(eng, m.evacuated, 2 * NB * t + j - 3)
                    w = slot_of(m.unit + j)
                    for n, (kt, (pw, px)) in enumerate((kt, q) for kt in range(NB) for q in three):
                        if j == 0 and n % 3 == 0:
                            eng.wait_ge(m.x_lo, NB * t + kt + 1)
                        x = (m.hi, m.lo)[px][tp]
                        mm = nc.tensor.matmul(m.banks[j % 4][:, 0:PT], w[pw][:, kt * P:(kt + 1) * P], x[:, kt, :],
                                              start=(n == 0), stop=(n == 3 * NB - 1))
                    mm.then_inc(m.proj_done, 1)
                    if j == 0:
                        eng.wait_ge(m.sq_added, NB * (t + 1))
                        need(eng, m.std_done, t)
                        nc.tensor.matmul(m.sum_bank[:, 0:PT], ones[:, :], m.acc[:, 0, :], start=True, stop=True)\
                          .then_inc(m.ms_done, 1)
                    after(s, j)
                    if m.heads and 2 <= j < NB + 2:
                        head_sum(t, j - 2)

            run_project(eng, m, body)

        VECTOR_UNITS = 4

        def load_unit(eng, u):
            need(eng, w_split, u - 1)
            eng.dma_start(raw[:, u % 2, :], A["weights"][u, :, :]).then_inc(raw_loaded[u % 2], 16)

        SLOTS_IN_B = (list(range(UNITS_GATE)) + list(range(UNITS_GATE + UNITS_KV, SLOTS_A + SLOTS_B))
                      + list(range(UNITS_GATE, UNITS_GATE + UNITS_KV)) + [SLOTS_A + SLOTS_B, SLOTS_A + SLOTS_B + 1])
        SLOTS_OUT_B = [k for k in SLOTS_IN_B if k < SLOTS_A]

        def slot_of(u):
            if u < U_GATE:
                return slot(u - U_A1, a1.extra)
            if u < U_B1:
                return slot(u - U_GATE)
            return slot(SLOTS_IN_B[u - U_B1], b1.extra) if u < U_OUT_B else slot(SLOTS_OUT_B[u - U_OUT_B])

        def high_part(eng, u, freed=None, count=0):
            eng.wait_ge(raw_loaded[u % 2], 16 * (u // 2 + 1))
            if freed is not None:
                eng.wait_ge(freed, count)
            nc.scalar.activation(slot_of(u)[0], raw[:, u % 2, :], ACT.Copy).then_inc(w_high, 1)

        def low_part(eng, ops, u):
            high, low = slot_of(u)
            eng.wait_ge(w_high, u + 1)
            ops.tensor_tensor(low, raw[:, u % 2, :], high.bitcast(F32), ALU.subtract).then_inc(w_split, 1)

        def low_units(eng, first, end):
            for u in range(first, end):
                if u >= VECTOR_UNITS:
                    low_part(eng, nc.gpsimd, u)
                if u + 2 < UNITS:
                    load_unit(eng, u + 2)

        def place(j):
            return 2 * (j // NB) + j % 2

        def stored_before(t, j):
            return 16 * (NB // 2 * t + j % NB // 2)

        def input_place(s, j):
            blk = j if isinstance(s, int) and s == 0 else j - 3
            return blk if known(s, 0, PN - 1) and 0 <= blk < NB else None

        def project_unit(m, s, j):
            if not isinstance(s, int):
                return None
            if m.first_weights and s == 0 and j in (0, 2, 4, 6, 8):
                return (m.unit + j // 2,)
            if m.first_weights and s == 1 and j + 5 < 2 * NB:
                return (m.unit + 5 + j,)
            if not m.first_weights and s == 1 and 1 <= j <= 7:
                return m.unit + 8 + j, r.kv_mm, NB * RN
            if s == PN and j:
                last_use = SLOTS_IN_B if m.heads else list(range(2 * NB))
                for k in range(m.next_units):
                    if j == last_use.index(SLOTS_OUT_B[k] if m.heads else k) + 1:
                        return m.unit + 2 * NB + k, m.proj_done, 2 * NB * (PN - 1) + j
            return None

        def recurrent_units(s, g):
            own = {(1, 1): 11, (1, 2): 12, (1, 3): 13}
            behind = {(RN, 0): (0, 1), (RN, 2): (2,), (RN, 3): (3, 4), (RN + 1, 0): (5,), (RN + 1, 1): (6, 7),
                      (RN + 1, 3): (8,)}
            if not isinstance(s, int):
                return []
            if (s, g) in own:
                return [(U_GATE + own[s, g], a1.proj_done, 2 * NB * PN)]
            out = []
            for k in behind.get((s, g), ()):
                if k < UNITS_GATE:
                    freed, count = r.gates_done, 4 * NG * RN
                else:
                    freed, count = r.out_done, NB * (RN - 1) + k - UNITS_GATE + 1
                out.append((U_B1 + k, freed, count))
            return out

        xc_src = A["xc"].rearrange("(b p) t -> p b t", p=P)
        sga_src = A["sga"].rearrange("(b p) t -> p b t", p=P)
        x_src = A["xT"].rearrange("(b p) t -> p b t", p=P)
        x1_dst = A["x1"].rearrange("(b p) t -> p b t", p=P)
        conv0 = A["conv0"].rearrange("(b p) t -> p b t", p=P)

        def back_pair(s, g):
            t, pair, lag = (s - 1, g - 2, 1) if g >= 2 else (s - 2, g + 2, 2)
            return (t, 2 * pair) if known(s, lag, RN - 1 + lag) else None

        EARLY = {(PN, 9): 0, (PN, 13): 1}

        def run_recurrent(eng, turn, last, after=None):
            def body(s, par):
                for g in range(NG):
                    if not (isinstance(s, int) and s == 0 and g < len(EARLY)):
                        turn(s, par, g)
                    if after:
                        after(s, g)
            run_steps(eng, 2, RN - 2, last, body)

        def ahead(s, par, g):
            if g < NG - 1:
                return (s, g + 1) if known(s, 0, RN - 1) else None
            return (s + 1, 0) if known(s, 0, RN - 2) else None

        def queries_inputs(s, g):
            at = {(RN, 2): (0,), (RN, 3): (1, 2), (RN + 1, 0): (3, 4), (RN + 1, 1): (5, 6, 7)}
            return at.get((s, g), ()) if isinstance(s, int) else ()

        def lagged(s, par, g, d):
            if g >= d:
                return (s, par, g - d) if known(s, 0, RN - 1) else None
            return (s - 1, 1 - par, g - d + NG) if known(s, 1, RN) else None

        def recurrent_sync(eng):
            def load_branch(s, g):
                need(eng, r.ix_done, NG * (s - 1) + g + 1)
                eng.dma_start(r.xc[:, g, :, :], xc_src[:, 2 * g:2 * g + 2, cols(s * RT, RT)])\
                   .then_inc(r.xc_loaded[g], 16)

            def load_gate(s, g):
                n, q = NG * s + g, g % 2
                need(eng, r.y_done, n - 1)
                eng.dma_start(r.sg[:, q, :, :], sga_src[:, 2 * g:2 * g + 2, cols(s * RT, RT)])\
                   .then_inc(r.sg_loaded[q], 16)

            def load_x(pair, q):
                t, blk = pair[0], pair[1] + q
                need(eng, r.x1_stored[q], 16 * (NB // 2 * t + blk // 2))
                need(eng, r.sq_done, NB * t + blk - 1)
                need(eng, r.x1_low, NB * t + blk - 1)
                eng.dma_start(r.x1[:, q, :], x_src[:, blk, cols(t * RT, RT)]).then_inc(r.x_loaded[q], 16)

            def store_x1(pair, q):
                t, blk = pair[0], pair[1] + q
                eng.wait_ge(r.resid_done, NB * t + blk + 1)
                eng.dma_start(x1_dst[:, blk, cols(t * RT, RT)], r.x1[:, q, :]).then_inc(r.x1_stored[q], 16)

            def body(s, par):
                for g in range(NG):
                    if isinstance(s, int) and (s, g) == (RN + 1, 3):
                        for stored in r.x1_stored:
                            eng.wait_ge(stored, 16 * RN * NB // 2)
                        eng.sem_inc(r.x1_free, 1)
                    pair = back_pair(s, g)
                    behind = back_pair(s, g + 1) if g < NG - 1 else back_pair(s + 1, 0)
                    if g < 2 and known(s, 1, RN - 1):
                        load_branch(s, g + 2)
                    if g >= 2 and known(s, 0, RN - 2):
                        load_branch(s + 1, g - 2)
                    if pair:
                        store_x1(pair, 0)
                    if known(s, 0, RN - 1) and not (isinstance(s, int) and s == 0 and g < 2):
                        load_gate(s, g)
                    if behind:
                        load_x(behind, 0)
                    if pair:
                        store_x1(pair, 1)
                    if behind:
                        load_x(behind, 1)
                    if known(s, 2, RN + 1) and g == 3:
                        t = s - 2
                        eng.wait_ge(r.kv_read, 2 * (t + 1))
                        eng.dma_start(A["v"][:, cols(t * RT, RT)], r.v[:, :]).then_inc(r.v_stored, 16)
                        eng.wait_ge(r.k_done, t + 1)
                        eng.dma_start(A["k"][:, cols(t * RT, RT)], r.k[:, :]).then_inc(r.k_stored, 16)
                    if isinstance(s, int) and (s, g) == (RN, 2):
                        eng.wait_ge(r.y_low, NG * RN)
                        for stored in r.x1_stored:
                            eng.wait_ge(stored, 16 * NB)
                        for blk in range(4):
                            load_input(eng, b1, 0, blk)
                    for blk in {(RN, 3): (4,), (RN + 1, 0): (5, 6), (RN + 1, 1): (7,)}.get((s, g), ()) \
                            if isinstance(s, int) else ():
                        load_input(eng, b1, 0, blk)

            def start():
                eng.wait_ge(a1.proj_done, 2 * NB * (PN - 1))
                for stored in a1.stored[0:2]:
                    eng.wait_ge(stored, 16 * NB // 2)
                for g in range(NG):
                    load_branch(0, g)

            def start_gates():
                eng.wait_ge(a1.ms_done, PN)
                eng.wait_ge(a1.halo_set, NB * PN)
                for stored in a1.stored[2:4]:
                    eng.wait_ge(stored, 16 * NB // 2)
                load_gate(0, 0)
                load_gate(0, 1)

            project_sync(eng, a1, {0: start, NB: start_gates})
            run_steps(eng, 2, RN - 2, RN + 2, body)
            for state, name in ((halo_sample, "conv_sample"), (halo, "conv_prompt")):
                eng.dma_start(A[name].rearrange("(b p) t -> p b t", p=P), state[:, :, :]).then_inc(misc_stored, 16)
            eng.wait_ge(r.h_kept, NG * RN)
            eng.dma_start(A["h_prompt"], h_last[:, :]).then_inc(misc_stored, 16)
            eng.dma_start(A["h_sample"], h_sample[:, :]).then_inc(misc_stored, 16)
            eng.wait_ge(misc_stored, 64)
            eng.wait_ge(r.v_stored, 16 * RN)
            eng.wait_ge(r.k_stored, 16 * RN)
            for i in range(2):
                eng.wait_ge(r.x1_stored[i], 16 * RN * NB // 2)
            eng.sem_inc(recurrent_stored, 1)

        def recurrent_vector(eng):
            def high(s, g):
                n, q = NG * s + g, g % 2
                eng.wait_ge(r.xc_loaded[g], 16 * (s + 1))
                need(eng, r.gates_done, 4 * (n - 1))
                nc.vector.tensor_copy(r.xc_hi[:, q, :, :], r.xc[:, g, :, :]).then_inc(r.xc_high, 1)

            def one_minus(s, par, g):
                n, q = NG * s + g, g % 2
                eng.wait_ge(r.a2_done, n + 1)
                nc.vector.scalar_tensor_tensor(out=r.th[:, q, :, :], in0=r.tr[:, q, :, :], scalar=1.0,
                                               in1=r.th[:, q, :, :], op0=ALU.add, op1=ALU.mult).then_inc(r.m2_done, 1)

            def gated_input(s, par, g):
                n, q = NG * s + g, g % 2
                eng.wait_ge(r.gates_read, 4 * n + 4)
                nc.vector.scalar_tensor_tensor(out=r.ti[:, q, :, :], in0=r.ti[:, q, :, :], scalar=1.0,
                                               in1=r.xc[:, g, :, :], op0=ALU.add, op1=ALU.mult).then_inc(r.ix_done, 1)

            def scan(s, par, g):
                n, q = NG * s + g, g % 2
                first = isinstance(s, int) and s == 0
                eng.wait_ge(r.bx_done, n + 1)
                need(eng, r.h_kept, n - NG + 1)
                for blk in range(2):
                    c = 2 * g + blk
                    if first:
                        nc.vector.tensor_tensor_scan(r.th[:, q, blk, 0:SAMPLE], r.a[:, q, blk, 0:SAMPLE],
                                                     r.ti[:, q, blk, 0:SAMPLE], vec[:, H0, c:c + 1],
                                                     ALU.mult, ALU.add)
                        i = nc.vector.tensor_tensor_scan(r.th[:, q, blk, SAMPLE:RT], r.a[:, q, blk, SAMPLE:RT],
                                                         r.ti[:, q, blk, SAMPLE:RT], 0.0, ALU.mult, ALU.add)
                    else:
                        i = nc.vector.tensor_tensor_scan(r.th[:, q, blk, :], r.a[:, q, blk, :], r.ti[:, q, blk, :],
                                                         h_last[:, c:c + 1], ALU.mult, ALU.add)
                    i.then_inc(r.scan_done, 1)
                eng.wait_ge(r.scan_done, 2 * n + 2)
                if first:
                    nc.vector.tensor_copy(h_sample[:, 2 * g:2 * g + 2], r.th[:, q, :, SAMPLE - 1])
                nc.vector.tensor_copy(h_last[:, 2 * g:2 * g + 2], r.th[:, q, :, RT - 1]).then_inc(r.h_kept, 1)

            def y_high(s, par, g):
                n, q = NG * s + g, g % 2
                eng.wait_ge(r.y_done, n + 1)
                need(eng, r.out_done, NB * (s - 1))
                nc.vector.tensor_copy(r.y_hi[par][:, 2 * g:2 * g + 2, :], r.th[:, q, :, :]).then_inc(r.y_high, 1)

            def residual(pair, q):
                t, blk = pair[0], pair[1] + q
                mth = NB * t + blk
                eng.wait_ge(r.out_done, mth + 1)
                eng.wait_ge(r.x_loaded[q], 16 * (NB // 2 * t + blk // 2 + 1))
                nc.vector.tensor_tensor(r.x1[:, q, :], bank[4 + q][:, 0:RT], r.x1[:, q, :], ALU.add)\
                  .then_inc(r.resid_done, 1)
                eng.wait_ge(r.resid_done, mth + 1)
                need(eng, r.kv_mm, mth - 1)
                nc.vector.tensor_scalar(r.x1_hi[:, q, :], r.x1[:, q, :], vec[:, G_KV, blk:blk + 1], None, ALU.mult)\
                  .then_inc(r.x1_high, 1)
                need(eng, r.sq_added, mth - 1)
                nc.vector.tensor_tensor(r.sq[:, q, :], r.x1[:, q, :], r.x1[:, q, :], ALU.mult).then_inc(r.sq_done, 1)
                eng.wait_ge(r.x1_high, mth + 1)
                nc.vector.scalar_tensor_tensor(out=r.x1_lo[:, q, :], in0=r.x1[:, q, :],
                                               scalar=vec[:, G_KV, blk:blk + 1], in1=r.x1_hi[:, q, :].bitcast(F32),
                                               op0=ALU.mult, op1=ALU.subtract).then_inc(r.x1_low, 1)

            def add_square(pair, q):
                t, blk = pair[0], pair[1] + q
                mth = NB * t + blk
                eng.wait_ge(r.sq_done, mth + 1)
                if blk == 0:
                    need(eng, r.ms_done, t)
                    nc.vector.tensor_copy(r.acc[:, :], r.sq[:, q, :]).then_inc(r.sq_added, 1)
                else:
                    eng.wait_ge(r.sq_added, mth)
                    nc.vector.tensor_tensor(r.acc[:, :], r.acc[:, :], r.sq[:, q, :], ALU.add).then_inc(r.sq_added, 1)

            def tail_read(t):
                eng.wait_ge(r.std_done, t + 1)
                need(eng, r.kv_read, 2 * t)
                nc.vector.reciprocal(r.rstd[:, :], r.std[:, :]).then_inc(r.rstd_done, 1)
                eng.wait_ge(r.rstd_done, t + 1)
                eng.wait_ge(r.kv_mm, NB * (t + 1))
                need(eng, r.k_stored, 16 * t)
                nc.vector.tensor_tensor(r.k[:, :], bank[6][:, 0:RT], r.rstd[:, :], ALU.mult).then_inc(r.kv_read, 1)
                need(eng, r.v_stored, 16 * t)
                nc.vector.tensor_tensor(r.v[:, :], bank[7][:, 0:RT], r.rstd[:, :], ALU.mult).then_inc(r.kv_read, 1)
                eng.wait_ge(r.kv_read, 2 * t + 1)
                need(eng, r.kms_done, t)
                nc.vector.tensor_tensor(r.k2[:, :], r.k[:, :], r.k[:, :], ALU.mult).then_inc(r.k2_done, 1)

            def tail_norm(t):
                eng.wait_ge(r.kstd_done, t + 1)
                nc.vector.reciprocal(r.std[:, :], r.std[:, :]).then_inc(r.krec_done, 1)
                eng.wait_ge(r.krec_done, t + 1)
                nc.vector.scalar_tensor_tensor(out=r.k[:, :], in0=r.k[:, :], scalar=vec[:, KN, 0:1], in1=r.std[:, :],
                                               op0=ALU.mult, op1=ALU.mult).then_inc(r.k_done, 1)

            def turn(s, par, g):
                one, two, pair = lagged(s, par, g, 1), lagged(s, par, g, 2), back_pair(s, g)
                if isinstance(s, int) and (s, g) == (0, 0):
                    high(0, 0)
                if ahead(s, par, g):
                    high(*ahead(s, par, g))
                if one:
                    one_minus(*one)
                if two:
                    scan(*two)
                if one:
                    gated_input(*one)
                if pair:
                    residual(pair, 0)
                if two:
                    y_high(*two)
                if known(s, 2, RN + 1) and g == 2:
                    tail_read(s - 2)
                if known(s, 2, RN + 1) and g == 3:
                    tail_norm(s - 2)
                if pair:
                    add_square(pair, 0)
                    residual(pair, 1)
                    add_square(pair, 1)

            def after_project(s, j):
                if isinstance(s, int) and (s, j) == (PN, NB):
                    decays(eng)
                if isinstance(s, int) and (s, j) in ((PN, 7), (PN, 12)):
                    turn(0, 0, 0 if j == 7 else 1)

            def after_slot(s, g):
                for blk in queries_inputs(s, g):
                    low_input(eng, b1, 0, 0, blk)

            project_vector(eng, a1, after_project)
            run_recurrent(eng, turn, RN + 2, after_slot)
            eng.wait_ge(r.x1_free, 1)

        def recurrent_scalar(eng):
            def multiplier(s, par, g):
                n, q = NG * s + g, g % 2
                eng.wait_ge(r.m2_done, n + 1)
                nc.scalar.activation(r.th[:, q, :, :], r.th[:, q, :, :], ACT.Sqrt, scale=0.25).then_inc(r.mult_done, 1)

            def gates(s, g):
                n, q = NG * s + g, g % 2
                need(eng, r.scan_done, 2 * (n - 1))
                for mat, dst in enumerate((r.ti, r.tr)):
                    for blk in range(2):
                        c = 2 * g + blk
                        eng.wait_ge(r.gates_done, 4 * n + 2 * mat + blk + 1)
                        nc.scalar.activation(dst[:, q, blk, :], bank[2 * mat + blk][:, 0:RT], ACT.Tanh, scale=0.5,
                                             bias=half_bias[:, mat, c:c + 1]).then_inc(r.gates_read, 1)
                eng.wait_ge(r.gates_read, 4 * n + 4)
                for blk in range(2):
                    c = 2 * g + blk
                    nc.scalar.activation(r.a[:, q, blk, :], r.tr[:, q, blk, :], ACT.Exp, scale=neg_decay[:, c:c + 1],
                                         bias=neg_decay[:, c:c + 1]).then_inc(r.decayed, 1)
                need(eng, r.y_low, n - 1)
                for blk in range(2):
                    c = 2 * g + blk
                    nc.scalar.activation(r.th[:, q, blk, :], r.tr[:, q, blk, :], ACT.Tanh, scale=decay[:, c:c + 1],
                                         bias=decay[:, c:c + 1]).then_inc(r.decayed, 1)
                eng.wait_ge(r.decayed, 4 * n + 4)
                nc.scalar.activation(r.tr[:, q, :, :], r.a[:, q, :, :], ACT.Square).then_inc(r.a2_done, 1)

            def turn(s, par, g):
                one, t = lagged(s, par, g, 1), s - 2
                if isinstance(s, int) and (s, g) == (0, 0):
                    eng.wait_ge(lw_step, LW_STEPS)
                if one:
                    multiplier(*one)
                if known(s, 2, RN + 1) and g == 2:
                    eng.wait_ge(r.ms_done, t + 1)
                    need(eng, r.k_done, t)
                    nc.scalar.activation(r.std[:, :], bank[5][:, 0:RT], ACT.Sqrt, scale=1.0 / D,
                                         bias=eps[:, 0:1]).then_inc(r.std_done, 1)
                if known(s, 2, RN + 1) and g == 3:
                    eng.wait_ge(r.rstd_done, t + 1)
                    eng.wait_ge(r.kms_done, t + 1)
                    nc.scalar.activation(r.std[:, :], bank[5][:, 0:RT], ACT.Sqrt, scale=1.0 / HEAD,
                                         bias=eps[:, 0:1]).then_inc(r.kstd_done, 1)
                if known(s, 0, RN - 1):
                    gates(s, g)
                for unit in recurrent_units(s, g):
                    high_part(eng, *unit)

            def after_project(s, j):
                if isinstance(s, int) and (s, j) in EARLY:
                    turn(0, 0, EARLY[s, j])

            def after_slot(s, g):
                for blk in queries_inputs(s, g):
                    high_input(eng, b1, 0, 0, blk)

            project_scalar(eng, a1, after_project)
            run_recurrent(eng, turn, RN + 2, after_slot)

        def recurrent_gpsimd(eng):
            def low(s, g):
                n, q = NG * s + g, g % 2
                eng.wait_ge(r.xc_high, n + 1)
                need(eng, r.gates_done, 4 * (n - 1))
                nc.gpsimd.tensor_tensor(r.xc_lo[:, q, :, :], r.xc[:, g, :, :],
                                        r.xc_hi[:, q, :, :].bitcast(F32), ALU.subtract).then_inc(r.xc_low, 1)

            def output(s, par, g):
                n, q = NG * s + g, g % 2
                eng.wait_ge(r.h_kept, n + 1)
                eng.wait_ge(r.sg_loaded[q], 16 * (2 * s + g // 2 + 1))
                nc.gpsimd.tensor_tensor(r.th[:, q, :, :], r.th[:, q, :, :], r.sg[:, q, :, :], ALU.mult)\
                  .then_inc(r.y_done, 1)
                eng.wait_ge(r.y_high, n + 1)
                nc.gpsimd.tensor_tensor(r.y_lo[par][:, 2 * g:2 * g + 2, :], r.th[:, q, :, :],
                                        r.y_hi[par][:, 2 * g:2 * g + 2, :].bitcast(F32), ALU.subtract)\
                  .then_inc(r.y_low, 1)

            def scan_input(s, par, g):
                n, q = NG * s + g, g % 2
                eng.wait_ge(r.ix_done, n + 1)
                eng.wait_ge(r.mult_done, n + 1)
                nc.gpsimd.tensor_tensor(r.ti[:, q, :, :], r.ti[:, q, :, :], r.th[:, q, :, :], ALU.mult)\
                  .then_inc(r.bx_done, 1)

            def turn(s, par, g):
                one, two = lagged(s, par, g, 1), lagged(s, par, g, 2)
                if isinstance(s, int) and (s, g) == (0, 0):
                    low(0, 0)
                if ahead(s, par, g):
                    low(*ahead(s, par, g))
                if two:
                    output(*two)
                if one:
                    scan_input(*one)

            low_units(eng, 0, U_GATE + 7)
            turn(0, 0, 0)
            low_units(eng, U_GATE + 7, U_GATE + 11)
            turn(0, 0, 1)

            def after_slot(s, g):
                if isinstance(s, int) and s < RN:
                    for unit in recurrent_units(s, g):
                        low_units(eng, unit[0], unit[0] + 1)

            run_recurrent(eng, turn, RN + 1, after_slot)

        def recurrent_tensor(eng):
            def gates(s, g):
                n, q = NG * s + g, g % 2
                eng.wait_ge(w_split, U_GATE + g + 1)
                eng.wait_ge(r.xc_low, n + 1)
                w, x = slot(g), (r.xc_hi, r.xc_lo)
                for mat in range(2):
                    for ob in range(2):
                        need(eng, r.gates_read, 4 * (n - 1) + 2 * mat + ob + 1)
                        for i, (kt, (pw, px)) in enumerate((kt, c) for kt in range(2) for c in three):
                            at = (mat * 2 + kt) * 2 * P + ob * P
                            mm = nc.tensor.matmul(bank[2 * mat + ob][:, 0:RT], w[pw][:, at:at + P],
                                                  x[px][:, q, kt, :], start=(i == 0), stop=(i == 5))
                        mm.then_inc(r.gates_done, 1)

            def kv(t, blk):
                mth = NB * t + blk
                eng.wait_ge(r.x1_low, mth + 1)
                if blk == 0:
                    need(eng, r.kv_read, 2 * t)
                    eng.wait_ge(w_split, U_KV + 2)
                for o in range(2):
                    w = slot(UNITS_GATE + o)
                    for i, (pw, px) in enumerate(three):
                        mm = nc.tensor.matmul(bank[6 + o][:, 0:RT], w[pw][:, blk * P:(blk + 1) * P],
                                              (r.x1_hi, r.x1_lo)[px][:, blk % 2, :],
                                              start=(blk == 0 and i == 0), stop=(blk == NB - 1 and i == 2))
                mm.then_inc(r.kv_mm, 1)

            def out(t, tp, blk):
                mth = NB * t + blk
                if blk == 0:
                    eng.wait_ge(r.y_low, NG * (t + 1))
                if blk == 1:
                    need(eng, r.std_done, t)
                if blk == 3:
                    need(eng, r.kstd_done, t)
                eng.wait_ge(w_split, U_OUT_A + blk + 1)
                need(eng, r.resid_done, mth - 1)
                w = slot(UNITS_GATE + UNITS_KV + blk)
                for i, (kt, (pw, px)) in enumerate((kt, c) for kt in range(NB) for c in three):
                    mm = nc.tensor.matmul(bank[4 + blk % 2][:, 0:RT], w[pw][:, kt * P:(kt + 1) * P],
                                          (r.y_hi, r.y_lo)[px][tp][:, kt, :], start=(i == 0), stop=(i == 3 * NB - 1))
                mm.then_inc(r.out_done, 1)

            def token_sum(t):
                eng.wait_ge(r.sq_added, NB * (t + 1))
                eng.wait_ge(r.resid_done, NB * (t + 1))
                nc.tensor.matmul(bank[5][:, 0:RT], ones[:, :], r.acc[:, :], start=True, stop=True)\
                  .then_inc(r.ms_done, 1)

            def key_sum(t, last):
                eng.wait_ge(r.k2_done, t + 1)
                if not last:
                    eng.wait_ge(r.resid_done, NB * (t + 1) + 2)
                nc.tensor.matmul(bank[5][:, 0:RT], head_ones[:, :], r.k2[:, :], start=True, stop=True)\
                  .then_inc(r.kms_done, 1)

            def turn(s, par, g):
                pair, tail = back_pair(s, g), known(s, 2, RN + 1)
                if isinstance(s, int) and (s, g) == (0, 0):
                    eng.wait_ge(a1.std_done, PN)
                if isinstance(s, int) and (s, g) == (1, 2):
                    eng.wait_ge(a1.evacuated, 2 * NB * PN)
                if pair:
                    tp = 1 - par if g >= 2 else par
                    out(pair[0], tp, pair[1])
                    if g != 2:
                        kv(pair[0], pair[1] - 1)
                if tail and g == 2:
                    kv(s - 2, NB - 1)
                    token_sum(s - 2)
                if tail and g == 3 and known(s, 2, RN):
                    key_sum(s - 2, False)
                if known(s, 0, RN - 1):
                    gates(s, g)
                if pair:
                    out(pair[0], tp, pair[1] + 1)
                    kv(pair[0], pair[1])

            def after_project(s, j):
                if isinstance(s, int) and (s, j) in EARLY:
                    turn(0, 0, EARLY[s, j])

            def after_queries(s, j):
                if isinstance(s, int) and (s, j) == (1, 0):
                    key_sum(RN - 1, True)

            project_tensor(eng, a1, after_project)
            run_recurrent(eng, turn, RN + 2)
            eng.wait_ge(r.gates_read, 4 * NG * RN)
            project_tensor(eng, b1, after_queries)

        q_src = A["qn"].rearrange("(b p) t -> p b t", p=P)
        sgb_src = A["sgb"].rearrange("(b p) t -> p b t", p=P)
        k_src = A["k"].rearrange("(n d) t -> d n t", d=HEAD)
        k0_src = A["k0"].rearrange("(n d) t -> d n t", d=HEAD)
        y_dst = A["yT"].rearrange("(b p) t -> p b t", p=P)
        LAST = AN + 1

        def unit_of(s, i):
            return i if isinstance(s, int) and s == 0 else 2 + 8 * (s - 1) + i

        def units(s):
            return 2 if isinstance(s, int) and s == 0 else 8

        def lagged_unit(s, par, i, d):
            if i >= d:
                return s, par, i - d
            if isinstance(s, int) and s == 0:
                return None
            return s - 1, 1 - par, units(s - 1) + i - d

        def out_bank(ts, blk):
            return bank[6] if isinstance(ts, int) and ts == AN and blk % 2 else bank[7]

        def out_block(s, i):
            if i < 2:
                return (s - 2, NB - 2 + i) if known(s, 3, LAST) else None
            return (s - 1, i - 2) if known(s, 2, LAST - 1) else None

        def attention_sync(eng):
            def tile(s, par, parts=range(4)):
                done = m.tile_loaded[par]
                if isinstance(s, int) and s == 0:
                    eng.dma_start(m.q[0][:, 0, :, :], q_src[:, :, 0:SAMPLE]).then_inc(done, 16)
                    for e in range(2):
                        half = m.k[0][e * HEAD:(e + 1) * HEAD, :, :]
                        eng.dma_start(half[:, :, 0:WINDOW], k0_src).then_inc(done, 16)
                        eng.dma_start(half[:, :, WINDOW:WINDOW + SAMPLE], k_src[:, :, 0:SAMPLE]).then_inc(done, 16)
                    eng.dma_start(m.vt[0][:, 0:WINDOW], A["v0"]).then_inc(done, 16)
                    eng.dma_start(m.vt[0][:, WINDOW:WINDOW + SAMPLE], A["v"][:, 0:SAMPLE]).then_inc(done, 16)
                    return
                at = (s - 1) * AT + SAMPLE
                if 0 in parts and not (isinstance(s, int) and s == 1):
                    need(eng, m.y_done, unit_of(s - 1, 0))
                first = isinstance(s, int) and s == 1
                w0, width = (WINDOW, AT) if first else (0, WINDOW + AT)
                for part in parts:
                    if part == 0:
                        for e in range(2):
                            eng.dma_start(m.k[par][e * HEAD:(e + 1) * HEAD, :, w0:w0 + width],
                                          k_src[:, :, cols(at - WINDOW + w0, width)]).then_inc(done, 16)
                    if part == 1:
                        eng.dma_start(m.vt[par][:, w0:w0 + width], A["v"][:, cols(at - WINDOW + w0, width)])\
                           .then_inc(done, 16)
                    for j in ((), (0,), (1, 2), (3,))[part]:
                        eng.dma_start(m.q[par][:, j, :, :], q_src[:, :, cols(at + j * CHUNK, CHUNK)])\
                           .then_inc(done, 16)

            def tile_gate(s, par):
                if isinstance(s, int) and s == 0:
                    eng.dma_start(m.sg[0][:, :, 0:SAMPLE], sgb_src[:, :, 0:SAMPLE]).then_inc(m.sg_loaded[0], 16)
                else:
                    eng.dma_start(m.sg[par][:, :, :], sgb_src[:, :, cols((s - 1) * AT + SAMPLE, AT)])\
                       .then_inc(m.sg_loaded[par], 16)

            def start():
                eng.wait_ge(b1.proj_done, 2 * NB * (PN - 1))
                eng.wait_ge(b1.x_lo, NB * PN)
                eng.wait_ge(b1.sq_done, NB * PN)
                for stored in b1.stored:
                    eng.wait_ge(stored, 16 * NB // 2)
                tile(0, 0)
                tile(1, 1)

            def body(s, par):
                for i in range(units(s)):
                    ob = out_block(s, i)
                    if ob:
                        load_residual(*ob)
                    if 1 <= i <= 4 and known(s, 1, AN - 1):
                        tile(s + 1, 1 - par, (i - 1,))
                    if i == 5 and known(s, 1, AN - 1):
                        tile_gate(s + 1, 1 - par)

            def load_residual(ts, blk):
                nth = NB * (ts - 1) + blk
                need(eng, m.added, nth - 1)
                eng.dma_start(m.xres[:, blk % 2, 0:AT], x1_dst[:, blk, cols((ts - 1) * AT + SAMPLE, AT)])\
                   .then_inc(m.xres_loaded[blk % 2], 16)

            project_sync(eng, b1, {0: start})
            eng.wait_ge(b1.proj_done, 2 * NB * PN)
            tile_gate(0, 0)
            tile_gate(1, 1)
            run_attention(eng, body)
            load_residual(AN - 1, 6)
            load_residual(AN - 1, 7)
            for blk in range(NB):
                need(eng, m.added, NB * (AN - 1) + blk - 1)
                eng.dma_start(m.xres[:, blk % 2, 0:AT], x1_dst[:, blk, TOTAL - AT:TOTAL])\
                   .then_inc(m.xres_loaded[blk % 2], 16)
                eng.dma_start(m.xres[:, blk % 2, AT:AT + SAMPLE], x1_dst[:, blk, 0:SAMPLE])\
                   .then_inc(m.xres_loaded[blk % 2], 16)
            for q in range(2):
                eng.wait_ge(m.stored[q], 16 * (4 * (AN - 1) + 8))
            eng.wait_ge(misc_stored, 160)

        def run_attention(eng, body):
            for s in range(4):
                body(s, s % 2)
            with eng.Fori(0, (AN - 4) // 2) as i:
                body(i * 2 + 4, 0)
                body(i * 2 + 5, 1)
            body(AN, 0)

        def loaded(eng, s, par):
            eng.wait_ge(m.tile_loaded[par], s * 56 + (112 if par == 0 else 56))

        def valid(s, i):
            return WINDOW - CHUNK * (i // 2) if isinstance(s, int) and s == 1 and i < 4 else 0

        def attention_tensor(eng):
            def scores(s, par, i):
                u, (j, n) = unit_of(s, i), divmod(i, 2)
                if i == 0:
                    eng.wait_ge(m.k_scaled, s + 1)
                need(eng, m.exp_done, 4 * (u - 1))
                v0 = valid(s, i)
                for e in range(2):
                    rows = slice(e * HEAD, (e + 1) * HEAD)
                    for bp in range(2):
                        blk = 4 * n + 2 * bp
                        mm = nc.tensor.matmul(s_banks[:, 2 * (i % 2) + e, bp * 192 + v0:(bp + 1) * 192],
                                              m.q[par][rows, j, blk:blk + 2, :].rearrange("p b t -> p (b t)"),
                                              m.k[par][rows, n, j * CHUNK + v0:j * CHUNK + 192],
                                              start=True, stop=True, skip_group_check=True)
                mm.then_inc(m.s_done, 1)

            def transpose_p(s, par, i):
                u = unit_of(s, i)
                eng.wait_ge(m.p_done, u + 1)
                need(eng, m.pta_done, u)
                need(eng, m.ptb_done, u)
                if i == 0:
                    eng.wait_ge(m.va_done, s + 1)
                    eng.wait_ge(m.vb_done, s + 1)
                for k in range(4):
                    nc.tensor.transpose(bank[4][:, k * P:(k + 1) * P], m.p[:, i % 2, k, 0:P], ident[:, :])
                for k in range(4):
                    mm = nc.tensor.transpose(bank[5][:, k * P:(k + 1) * P], m.p[:, i % 2, k, CHUNK:192], ident[:, :])
                mm.then_inc(m.t_done, 1)

            def transpose_v(s, par):
                before = unit_of(s, 0)
                need(eng, m.pta_done, before)
                need(eng, m.ptb_done, before)
                loaded(eng, s, par)
                if isinstance(s, int) and s == 1:
                    eng.wait_ge(m.v_zero, 1)
                pairs = 2 if isinstance(s, int) and s == 0 else 5
                for k in range(min(pairs, 4)):
                    nc.tensor.transpose(bank[4][:, k * P:(k + 1) * P], m.vt[par][:, k * CHUNK:k * CHUNK + P], ident[:, :])
                k = pairs - 1
                nc.tensor.transpose(bank[5][:, 0:P], m.vt[par][:, k * CHUNK:k * CHUNK + P], ident[:, :])\
                  .then_inc(m.vt_done, 1)

            def values(s, par, i):
                u, (j, n) = unit_of(s, i), divmod(i, 2)
                eng.wait_ge(m.pta_done, u + 1)
                eng.wait_ge(m.ptb_done, u + 1)
                eng.wait_ge(m.va_done, s + 1)
                eng.wait_ge(m.vb_done, s + 1)
                need(eng, m.y_done, u)
                for e in range(2):
                    out = bank[6][e * HEAD:(e + 1) * HEAD, 0:AT]
                    nc.tensor.matmul(out, m.v[par][:, j, n * HEAD:(n + 1) * HEAD], m.pt_a[:, e * AT:(e + 1) * AT],
                                     start=True, stop=False, skip_group_check=True)
                    mm = nc.tensor.matmul(out, m.v[par][HEAD:P, j + 1, n * HEAD:(n + 1) * HEAD],
                                          m.pt_b[HEAD:P, e * AT:(e + 1) * AT], start=False, stop=True,
                                          skip_group_check=True)
                mm.then_inc(m.pv_done, 1)

            def output(ts, tp, blk, width):
                nth = NB * (ts - 1) + blk
                last = isinstance(ts, int) and ts == AN
                eng.wait_ge(w_split, U_OUT_B + blk + 1)
                eng.wait_ge(m.y_low, 2 + 8 * ts)
                need(eng, m.added, nth - 1 if last and blk else nth)
                w = slot_of(U_OUT_B + blk)
                for n, (kt, (pw, px)) in enumerate((kt, c) for kt in range(NB) for c in three):
                    mm = nc.tensor.matmul(out_bank(ts, blk)[:, 0:width], w[pw][:, kt * P:(kt + 1) * P],
                                          (m.y_hi, m.y_lo)[px][tp][:, kt, 0:width], start=(n == 0),
                                          stop=(n == 3 * NB - 1))
                mm.then_inc(m.out_done, 1)

            def body(s, par):
                for i in range(units(s)):
                    one, two, ob = lagged_unit(s, par, i, 1), lagged_unit(s, par, i, 2), out_block(s, i)
                    scores(s, par, i)
                    if two:
                        values(*two)
                    if one:
                        transpose_p(*one)
                    if ob:
                        output(ob[0], par if i < 2 else 1 - par, ob[1], AT)
                    if i == 0:
                        transpose_v(s, par)

            eng.wait_ge(b1.evacuated, 2 * NB * PN)
            run_attention(eng, body)
            s, par = LAST, LAST % 2
            for i in range(2):
                values(*lagged_unit(s, par, i, 2))
                if i == 0:
                    transpose_p(*lagged_unit(s, par, i, 1))
                output(s - 2, par, NB - 2 + i, AT)
            for blk in range(NB):
                output(s - 1, 1 - par, blk, AT + SAMPLE)

        def attention_vector(eng):
            def scale_keys(s, par):
                loaded(eng, s, par)
                w0, w1 = (0, WINDOW + SAMPLE) if isinstance(s, int) and s == 0 else (0, WINDOW + AT)
                if isinstance(s, int) and s == 1:
                    w0 = WINDOW
                nc.vector.tensor_scalar(m.k[par][:, :, w0:w1], m.k[par][:, :, w0:w1], kq_scale[:, 0:1], None,
                                        ALU.mult).then_inc(m.k_scaled, 1)

            def maximum(s, par, i):
                u, q, n = unit_of(s, i), i % 2, i % 2
                v0 = valid(s, i)
                if v0 and i < 2:
                    eng.wait_ge(m.t_done, u - 1)
                    nc.vector.memset(m.p[:, q, :, 0:WINDOW], 0.0).then_inc(m.p_zero, 1)
                eng.wait_ge(m.s_done, u + 1)
                pair = s_banks[:, 2 * q:2 * q + 2, 0:384].rearrange("p e (b k) -> p e b k", b=2)
                nc.vector.tensor_reduce(m.nmax[:, q, :].rearrange("p (e b) -> p e b", e=2), pair[:, :, :, v0:192],
                                        AX.X, ALU.max, negate=True).then_inc(m.max_done, 1)
                eng.wait_ge(m.max_done, u + 1)
                need(eng, m.exp_done, 4 * (u - 1))
                nc.vector.tensor_tensor(m.nm[:, q, :], m.nmax[:, q, :], neg_sink[:, 4 * n:4 * n + 4], ALU.min)\
                  .then_inc(m.nm_done, 1)
                eng.wait_ge(m.nm_done, u + 1)
                need(eng, m.es_done, u - 1)
                nc.vector.tensor_tensor(m.sm[:, q, :], m.nm[:, q, :], sink[:, 4 * n:4 * n + 4], ALU.add)\
                  .then_inc(m.sm_done, 1)

            def normalise(s, par, i):
                u, q = unit_of(s, i), i % 2
                eng.wait_ge(m.exp_done, 4 * u + 4)
                eng.wait_ge(m.es_done, u + 1)
                nc.vector.tensor_tensor(m.dsum[:, q, :], m.den[:, q, :], m.es[:, q, :], ALU.add).then_inc(m.dsum_done, 1)
                eng.wait_ge(m.dsum_done, u + 1)
                nc.vector.reciprocal(m.rden[:, q, :], m.dsum[:, q, :]).then_inc(m.rden_done, 1)
                eng.wait_ge(m.rden_done, u + 1)
                for k in range(4):
                    op = nc.vector.tensor_scalar(m.p[:, q, k, :], m.p[:, q, k, :], m.rden[:, q, k:k + 1], None, ALU.mult)
                op.then_inc(m.p_done, 1)

            def read_pt_b(s, i):
                u = unit_of(s, i)
                eng.wait_ge(m.t_done, u + 1)
                need(eng, m.pv_done, u)
                nc.vector.tensor_copy(m.pt_b[HEAD:P, :], bank[5][HEAD:P, :]).then_inc(m.ptb_done, 1)

            def read_v(s, par):
                pairs = 2 if isinstance(s, int) and s == 0 else 5
                eng.wait_ge(m.vt_done, s + 1)
                nc.vector.tensor_copy(m.v[par][:, pairs - 1, :], bank[5][:, 0:P]).then_inc(m.vb_done, 1)

            def gate(s, par, i):
                u, (j, n), q = unit_of(s, i), divmod(i, 2), i % 2
                eng.wait_ge(m.pv_done, u + 1)
                need(eng, m.y_low, u - 1)
                eng.wait_ge(m.sg_loaded[par], s * 8 + (16 if par == 0 else 8))
                c0 = j * CHUNK
                nc.vector.tensor_tensor(m.y[:, q, :, :], bank[6][:, 0:AT].rearrange("p (b t) -> p b t", b=4),
                                        m.sg[par][:, 4 * n:4 * n + 4, c0:c0 + CHUNK], ALU.mult).then_inc(m.y_done, 1)
                eng.wait_ge(m.y_done, u + 1)
                dst = y_part(m.y_hi, s, par, i)
                nc.vector.tensor_copy(dst, m.y[:, q, :, :]).then_inc(m.y_high, 1)

            def add(ts, blk, width):
                nth, q = NB * (ts - 1) + blk, blk % 2
                eng.wait_ge(m.out_done, nth + 1)
                eng.wait_ge(m.xres_loaded[q], residual_count(ts, blk))
                each = 2 if isinstance(ts, int) and ts == AN else 1
                need(eng, m.stored[q], 16 * (4 * (ts - 1) + each * (blk // 2)))
                nc.vector.tensor_tensor(m.out[:, q, 0:width], out_bank(ts, blk)[:, 0:width], m.xres[:, q, 0:width], ALU.add)\
                  .then_inc(m.added, 1)

            def body(s, par):
                for i in range(units(s)):
                    one, two, ob = lagged_unit(s, par, i, 1), lagged_unit(s, par, i, 2), out_block(s, i)
                    maximum(s, par, i)
                    if two:
                        gate(*two)
                    if one:
                        read_pt_b(one[0], one[2])
                    normalise(s, par, i)
                    if ob:
                        add(ob[0], ob[1], AT)
                    if i == 0:
                        read_v(s, par)
                    if i == units(s) - 2 and known(s, 0, AN - 1):
                        scale_keys(s + 1, 1 - par)

            def after_project(s, j):
                if isinstance(s, int) and (s, j) == (PN, 12):
                    loaded(eng, 1, 1)
                    nc.vector.memset(m.vt[1][:, 0:WINDOW], 0.0).then_inc(m.v_zero, 1)
                    scale_keys(0, 0)

            project_vector(eng, b1, after_project)
            run_attention(eng, body)
            s, par = LAST, LAST % 2
            one = lagged_unit(s, par, 0, 1)
            gate(*lagged_unit(s, par, 0, 2))
            read_pt_b(one[0], one[2])
            add(s - 2, NB - 2, AT)
            gate(*one)
            add(s - 2, NB - 1, AT)
            for blk in range(NB):
                add(s - 1, blk, AT + SAMPLE)

        def y_part(parts, s, par, i):
            j, n = divmod(i, 2)
            if isinstance(s, int) and s == 0:
                return parts[AN % 2][:, 4 * n:4 * n + 4, AT:AT + SAMPLE]
            return parts[par][:, 4 * n:4 * n + 4, j * CHUNK:(j + 1) * CHUNK]

        def residual_count(ts, blk):
            if isinstance(ts, int) and ts == AN:
                return 16 * (4 * (AN - 1) + 2 * (blk // 2 + 1))
            return 16 * (4 * (ts - 1) + blk // 2 + 1)

        def attention_scalar(eng):
            def store(ts, blk, width):
                nth = NB * (ts - 1) + blk
                eng.wait_ge(m.added, nth + 1)
                eng.dma_start(y_dst[:, blk, cols((ts - 1) * AT + SAMPLE, AT)], m.out[:, blk % 2, 0:AT])\
                   .then_inc(m.stored[blk % 2], 16)
                if width > AT:
                    eng.dma_start(y_dst[:, blk, 0:SAMPLE], m.out[:, blk % 2, AT:width]).then_inc(m.stored[blk % 2], 16)

            def exps(s, i):
                u, q = unit_of(s, i), i % 2
                v0 = valid(s, i)
                eng.wait_ge(m.nm_done, u + 1)
                need(eng, m.t_done, u - 1)
                if v0 and i < 2:
                    eng.wait_ge(m.p_zero, i + 1)
                for e in range(2):
                    for bp in range(2):
                        k = 2 * e + bp
                        nc.scalar.activation(m.p[:, q, k, v0:192],
                                             s_banks[:, 2 * q + e, bp * 192 + v0:(bp + 1) * 192], ACT.Exp,
                                             bias=m.nm[:, q, k:k + 1], accum_out=m.den[:, q, k:k + 1])\
                          .then_inc(m.exp_done, 1)
                eng.wait_ge(m.sm_done, u + 1)
                nc.scalar.activation(m.es[:, q, :], m.sm[:, q, :], ACT.Exp).then_inc(m.es_done, 1)

            def read_pt_a(s, i):
                u = unit_of(s, i)
                eng.wait_ge(m.t_done, u + 1)
                need(eng, m.pv_done, u)
                nc.scalar.activation(m.pt_a[:, :], bank[4][:, :], ACT.Copy).then_inc(m.pta_done, 1)

            def read_v(s, par):
                n = 1 if isinstance(s, int) and s == 0 else 4
                eng.wait_ge(m.vt_done, s + 1)
                nc.scalar.activation(m.v[par][:, 0:n, :], bank[4][:, 0:n * P].rearrange("p (a b) -> p a b", a=n),
                                     ACT.Copy).then_inc(m.va_done, 1)

            def body(s, par):
                for i in range(units(s)):
                    one = lagged_unit(s, par, i, 1)
                    exps(s, i)
                    if one:
                        read_pt_a(one[0], one[2])
                    ob = out_block(s, i)
                    if ob:
                        store(ob[0], ob[1], AT)
                    if i == 0:
                        read_v(s, par)

            run_attention(eng, body)
            s, par = LAST, LAST % 2
            one = lagged_unit(s, par, 0, 1)
            read_pt_a(one[0], one[2])
            store(s - 2, NB - 2, AT)
            store(s - 2, NB - 1, AT)
            for blk in range(NB):
                store(s - 1, blk, AT + SAMPLE)

        def attention_gpsimd(eng):
            def low(s, par, i):
                u, q = unit_of(s, i), i % 2
                eng.wait_ge(m.y_high, u + 1)
                nc.gpsimd.tensor_tensor(y_part(m.y_lo, s, par, i), m.y[:, q, :, :],
                                        y_part(m.y_hi, s, par, i).bitcast(F32), ALU.subtract).then_inc(m.y_low, 1)

            run_attention(eng, lambda s, par: [low(s, par, i) for i in range(units(s))])

        block = stack.enter_context(nc.Block())

        @block.sync
        def _(eng):
            nc.disable_value_cache = True
            eng.dma_start(vec[:, :, :], A["vec"]).then_inc(const_loaded, 16)
            eng.dma_start(sink[:, :], A["sinks"]).then_inc(const_loaded, 16)
            eng.dma_start(halo[:, :, :], conv0).then_inc(const_loaded, 16)
            recurrent_sync(eng)
            eng.dma_start(A["k_prompt"], A["k"][:, TOTAL - WINDOW:TOTAL]).then_inc(misc_stored, 16)
            eng.dma_start(A["v_prompt"], A["v"][:, TOTAL - WINDOW:TOTAL]).then_inc(misc_stored, 16)
            eng.dma_start(A["k_sample"][:, 0:WINDOW - SAMPLE], A["k0"][:, SAMPLE:WINDOW]).then_inc(misc_stored, 16)
            eng.dma_start(A["k_sample"][:, WINDOW - SAMPLE:WINDOW], A["k"][:, 0:SAMPLE]).then_inc(misc_stored, 16)
            eng.dma_start(A["v_sample"][:, 0:WINDOW - SAMPLE], A["v0"][:, SAMPLE:WINDOW]).then_inc(misc_stored, 16)
            eng.dma_start(A["v_sample"][:, WINDOW - SAMPLE:WINDOW], A["v"][:, 0:SAMPLE]).then_inc(misc_stored, 16)
            attention_sync(eng)
            nc.disable_value_cache = False

        @block.gpsimd
        def _(eng):
            load_unit(eng, 0)
            load_unit(eng, 1)
            nc.gpsimd.memset(ident[:, :], 0.0).then_inc(const_pool, 1)
            eng.wait_ge(const_pool, 1)
            nc.gpsimd.affine_select(out=ident[:, :], in_=ident[:, :], compare_op=ALU.not_equal, fill=1.0, base=0,
                                    pattern=[[-1, P]], channel_multiplier=1).then_inc(const_pool, 1)
            recurrent_gpsimd(eng)
            low_units(eng, U_B1, UNITS)
            attention_gpsimd(eng)

        @block.scalar
        def _(eng):
            eng.wait_ge(const_loaded, 16 * N_CONST)
            nc.scalar.activation(lw[:, 0, :], vec[:, LAM, :], ACT.Abs).then_inc(lw_act, 1)
            eng.wait_ge(lw_act, 1)
            nc.scalar.activation(lw[:, 1, :], lw[:, 0, :], ACT.Exp, scale=-1.0).then_inc(lw_act, 1)
            eng.wait_ge(const_made, 3)
            recurrent_scalar(eng)
            project_scalar(eng, b1, nothing)
            attention_scalar(eng)

        @block.vector
        def _(eng):
            nc.vector.memset(eps[:, :], EPS).then_inc(const_made, 1)
            nc.vector.memset(ones[:, :], 1.0).then_inc(const_made, 1)
            nc.vector.memset(head_ones[:, :], 0.0).then_inc(const_made, 1)
            eng.wait_ge(const_made, 3)
            for e in range(2):
                nc.vector.memset(head_ones[e * HEAD:(e + 1) * HEAD, e * HEAD:(e + 1) * HEAD], 1.0)\
                  .then_inc(const_made, 1)
            eng.wait_ge(const_loaded, 16 * N_CONST)
            nc.vector.tensor_scalar(neg_sink[:, :], sink[:, :], -1.0, None, ALU.mult).then_inc(const_made, 1)
            nc.vector.tensor_scalar(kq_scale[:, :], vec[:, QN, 0:1], HEAD ** -0.5, None, ALU.mult)\
              .then_inc(const_made, 1)
            nc.vector.tensor_scalar(half_bias[:, :, :], vec[:, B_X:B_A + 1, :], 0.5, None, ALU.mult)\
              .then_inc(const_made, 1)
            recurrent_vector(eng)
            attention_vector(eng)

        @block.tensor
        def _(eng):
            eng.wait_ge(const_made, 5)
            eng.wait_ge(const_pool, 2)
            recurrent_tensor(eng)
            attention_tensor(eng)


INPUTS = {"xT": (D, TOTAL), "conv0": (D, HALO), "k0": (P, WINDOW), "v0": (P, WINDOW),
          "weights": (UNITS, P, D), "vec": (P, 16, NB), "sinks": (P, 8)}
OUTPUTS = {"yT": (D, TOTAL), "conv_prompt": (D, HALO), "conv_sample": (D, HALO), "h_prompt": (P, NB),
           "h_sample": (P, NB), "k_prompt": (P, WINDOW), "v_prompt": (P, WINDOW), "k_sample": (P, WINDOW),
           "v_sample": (P, WINDOW)}
SCRATCH = {"xc": (D, TOTAL), "sga": (D, TOTAL), "x1": (D, TOTAL), "qn": (D, TOTAL), "sgb": (D, TOTAL),
           "k": (P, TOTAL), "v": (P, TOTAL)}


def layout(inputs):
    import numpy as np
    g = {k: np.asarray(v) for k, v in inputs.items()}

    def columns(w):
        n = w.shape[1] // P
        return w.reshape(NB, P, n, P).transpose(2, 1, 0, 3).reshape(n, P, D)

    gates = np.stack([g["w_gate_x"][0], g["w_gate_a"][0]], 1)
    gates = gates.reshape(NG, 2, 2, P, 2 * P).transpose(0, 3, 1, 2, 4).reshape(NG, P, D)
    weights = np.concatenate([columns(g["w_in_a"][0]), gates, columns(g["w_kv"]), columns(g["w_out_a"][0]),
                              columns(g["w_in_b"][0]), columns(g["w_out_b"][0])], 0)

    def blocks(v):
        return v.reshape(NB, P).T

    def heads(v):
        return np.tile(np.tile(v, 2)[:, None], (1, NB))

    vec = np.stack([blocks(g["norm_a"][0]), blocks(g["norm_kv"]), blocks(g["norm_b"][0]), blocks(g["b_gate_x"][0]),
                    blocks(g["b_gate_a"][0]), blocks(g["lru_lambda"][0]), blocks(g["conv_b"][0]),
                    blocks(g["state_rglru"][0, 0]), heads(g["k_norm"]), heads(g["q_norm"][0])]
                   + [blocks(g["conv_w"][0, j]) for j in range(CONV)] + [blocks(g["norm_a"][0])] * 2, 1)
    sinks = g["sinks"][0].reshape(2, 2, 2, 2).transpose(2, 0, 3, 1).reshape(2, 8)
    return {
        "xT": np.ascontiguousarray(np.concatenate([g["x_sample"][0], g["x_prompt"][0]], 0).T),
        "conv0": np.ascontiguousarray(g["state_conv"][0, 0].T),
        "k0": np.ascontiguousarray(g["cache_k_win"][0].reshape(WINDOW, P).T),
        "v0": np.ascontiguousarray(g["cache_v_win"][0].reshape(WINDOW, P).T),
        "weights": np.ascontiguousarray(weights),
        "vec": np.ascontiguousarray(vec),
        "sinks": np.ascontiguousarray(np.repeat(sinks, HEAD, 0)),
    }


def program(nc):
    aps = {}
    for kind, group in (("ExternalInput", INPUTS), ("ExternalOutput", OUTPUTS), ("Internal", SCRATCH)):
        for name, shape in group.items():
            aps[name] = nc.dram_tensor(f"{name}_dram", shape, F32, kind=kind).ap()
    build(nc, aps)


def kernel(**inputs):
    import numpy as np
    import concourse.bacc as bacc
    from concourse.bass_utils import run_bass_kernel_spmd
    arrays = layout(inputs)
    nc = bacc.Bacc("TRN2", target_bir_lowering=False, num_devices=1)
    program(nc)
    result = run_bass_kernel_spmd(nc, [{f"{k}_dram": v for k, v in arrays.items()}], core_ids=[0]).results[0]
    o = {k: np.asarray(result[f"{k}_dram"]) for k in OUTPUTS}
    y = np.ascontiguousarray(o["yT"].T)

    def rows(a):
        return np.ascontiguousarray(a.T)[None, None]

    def state(a):
        return np.ascontiguousarray(a.T).reshape(1, 1, D)

    def window(a):
        return np.ascontiguousarray(a.T).reshape(1, WINDOW, 2, HEAD)

    return (y[None, SAMPLE:], y[None, :SAMPLE], rows(o["conv_prompt"]), state(o["h_prompt"]),
            window(o["k_prompt"]), window(o["v_prompt"]), rows(o["conv_sample"]), state(o["h_sample"]),
            window(o["k_sample"]), window(o["v_sample"]))
```
